# Optimizing a Trainium2 kernel written in Bass

```python
import math
import jax, jax.numpy as jnp
from jax import lax
import numpy as np

D_MODEL = 2048
BATCH = 1
SEQ = 256
DEPTH = 1
DEC_BATCH = 8
DEC_SEQ = 16
PAST_LEN = 128

CHUNK = 64
HEAD_DIM = 128
FOX_HEADS = 8
FOX_WIDTH = FOX_HEADS * HEAD_DIM
GDN_HEADS = 8
GDN_DK = 128
GDN_DV = 128
GDN_QK_WIDTH = GDN_HEADS * GDN_DK
GDN_V_WIDTH = GDN_HEADS * GDN_DV
GDN_CONV_CH = 2 * GDN_QK_WIDTH + GDN_V_WIDTH
CONV_W = 4
MIX_WIDTH = FOX_WIDTH + GDN_V_WIDTH
IN_SPLITS = (FOX_WIDTH, FOX_WIDTH, FOX_WIDTH, FOX_HEADS,
             GDN_QK_WIDTH, GDN_QK_WIDTH, GDN_V_WIDTH, GDN_HEADS, GDN_HEADS, GDN_V_WIDTH)
IN_COLS = sum(IN_SPLITS)
QBLK = 128
D_FF = ((8 * D_MODEL + 3 * 256 - 1) // (3 * 256)) * 256
DEEPNORM_ALPHA = (2 * DEPTH) ** 0.25
DEEPNORM_BETA = (8 * DEPTH) ** -0.25
FGATE_BIAS_MEAN = 2.0
DT_MIN = 0.001
DT_MAX = 0.1
LN_EPS = 1e-5
RMS_EPS = 1e-6
L2_EPS = 1e-6

kernel_name = 'hybrid_fox_gdn_streaming_encoder_step'

def layer_norm(x, g, b):
    xf = x.astype(jnp.float32)
    mu = jnp.mean(xf, axis=-1, keepdims=True)
    var = jnp.mean(jnp.square(xf - mu), axis=-1, keepdims=True)
    y = (xf - mu) * lax.rsqrt(var + LN_EPS) * g.astype(jnp.float32) + b.astype(jnp.float32)
    return y.astype(x.dtype)

def rms_norm(x, g):
    xf = x.astype(jnp.float32)
    y = xf * lax.rsqrt(jnp.mean(jnp.square(xf), axis=-1, keepdims=True) + RMS_EPS) * g.astype(jnp.float32)
    return y.astype(x.dtype)

def l2_normalize(x):
    xf = x.astype(jnp.float32)
    return xf * lax.rsqrt(jnp.sum(jnp.square(xf), axis=-1, keepdims=True) + L2_EPS)

def fox_block(q, c_q, pos_q, k, v, c_k, pos_k):
    s = jnp.einsum('bqhd,bkhd->bhqk', q, k).astype(jnp.float32) * (HEAD_DIM ** -0.5)
    s = s + jnp.transpose(c_q, (0, 2, 1))[..., :, None] - jnp.transpose(c_k, (0, 2, 1))[..., None, :]
    mask = pos_q[:, None] >= pos_k[None, :]
    s = jnp.where(mask, s, -jnp.inf)
    p = jax.nn.softmax(s, axis=-1).astype(v.dtype)
    return jnp.einsum('bhqk,bkhd->bqhd', p, v)

def fox_prompt(q, k, v, logf):
    bsz, t_ = q.shape[:2]
    c = jnp.cumsum(logf, axis=1)
    pos = jnp.arange(t_)
    nb = t_ // QBLK
    qb = q.reshape(bsz, nb, QBLK, FOX_HEADS, HEAD_DIM).transpose(1, 0, 2, 3, 4)
    cb = c.reshape(bsz, nb, QBLK, FOX_HEADS).transpose(1, 0, 2, 3)
    pb = pos.reshape(nb, QBLK)
    out = lax.map(lambda xs: fox_block(xs[0], xs[1], xs[2], k, v, c, pos), (qb, cb, pb))
    return out.transpose(1, 0, 2, 3, 4).reshape(bsz, t_, FOX_HEADS, HEAD_DIM)

def fox_sample(q, k_new, v_new, logf_new, k_cache, v_cache, logf_cache):
    past = k_cache.shape[1]
    t_ = q.shape[1]
    k = jnp.concatenate([k_cache.astype(k_new.dtype), k_new], axis=1)
    v = jnp.concatenate([v_cache.astype(v_new.dtype), v_new], axis=1)
    c = jnp.cumsum(jnp.concatenate([logf_cache.astype(jnp.float32), logf_new], axis=1), axis=1)
    pos_k = jnp.arange(past + t_)
    pos_q = past + jnp.arange(t_)
    return fox_block(q, c[:, past:], pos_q, k, v, c, pos_k)

def gated_delta_rule(q, k, v, g, beta, s0):
    bsz, t_, nh, dk = q.shape
    dv = v.shape[-1]
    lc = min(t_, CHUNK)
    n = t_ // lc

    def chunks(x):
        return x.reshape(bsz, n, lc, nh, x.shape[-1]).transpose(1, 0, 3, 2, 4)

    qc = chunks(q) * (dk ** -0.5)
    kc = chunks(k)
    vc = chunks(v.astype(jnp.float32))
    gc = chunks(g[..., None])[..., 0]
    bc = chunks(beta[..., None])[..., 0]
    gcum = jnp.cumsum(gc, axis=-1)
    tril = jnp.tril(jnp.ones((lc, lc), dtype=bool))
    strict = jnp.tril(jnp.ones((lc, lc), dtype=bool), k=-1)
    decay = jnp.exp(jnp.where(tril, gcum[..., :, None] - gcum[..., None, :], -jnp.inf))
    kb = kc * bc[..., None]
    a = jnp.where(strict, jnp.einsum('nbhid,nbhjd->nbhij', kb, kc) * decay, 0.0)
    ia = a + jnp.eye(lc, dtype=jnp.float32)
    u = lax.linalg.triangular_solve(ia, vc * bc[..., None], left_side=True, lower=True, unit_diagonal=True)
    w = lax.linalg.triangular_solve(ia, kb * jnp.exp(gcum)[..., None], left_side=True, lower=True,
                                    unit_diagonal=True)
    qk = jnp.einsum('nbhid,nbhjd->nbhij', qc, kc) * decay

    def step(s, xs):
        q_i, k_i, u_i, w_i, g_i, qk_i = xs
        v_new = u_i - jnp.einsum('bhld,bhdv->bhlv', w_i, s)
        o_i = (jnp.einsum('bhld,bhdv->bhlv', q_i * jnp.exp(g_i)[..., None], s)
               + jnp.einsum('bhij,bhjv->bhiv', qk_i, v_new))
        g_last = g_i[..., -1:]
        s = s * jnp.exp(g_last)[..., None] + jnp.einsum(
            'bhld,bhlv->bhdv', k_i * jnp.exp(g_last - g_i)[..., None], v_new)
        return s, o_i

    s_fin, o = lax.scan(step, s0.astype(jnp.float32), (qc, kc, u, w, gcum, qk))
    o = o.transpose(1, 0, 3, 2, 4).reshape(bsz, t_, nh, dv)
    return o, s_fin

def gdn_mixer(q_raw, k_raw, v_raw, a_raw, b_raw, z_raw, conv_buf, s0, conv_w, a_log, dt_bias, norm_w):
    bsz, t_ = q_raw.shape[:2]
    qkv = jnp.concatenate([q_raw, k_raw, v_raw], axis=-1)
    ext = jnp.concatenate([conv_buf.astype(qkv.dtype), qkv], axis=1)
    new_buf = ext[:, ext.shape[1] - (CONV_W - 1):]
    conv = ext[:, 0:t_] * conv_w[0]
    for i in range(1, CONV_W):
        conv = conv + ext[:, i:i + t_] * conv_w[i]
    conv = jax.nn.silu(conv)
    q = l2_normalize(conv[..., :GDN_QK_WIDTH].reshape(bsz, t_, GDN_HEADS, GDN_DK))
    k = l2_normalize(conv[..., GDN_QK_WIDTH:2 * GDN_QK_WIDTH].reshape(bsz, t_, GDN_HEADS, GDN_DK))
    v = conv[..., 2 * GDN_QK_WIDTH:].reshape(bsz, t_, GDN_HEADS, GDN_DV)
    g = -jnp.exp(a_log.astype(jnp.float32)) * jax.nn.softplus(
        a_raw.astype(jnp.float32) + dt_bias.astype(jnp.float32))
    beta = jax.nn.sigmoid(b_raw.astype(jnp.float32))
    o, s_fin = gated_delta_rule(q, k, v, g, beta, s0)
    z = z_raw.reshape(bsz, t_, GDN_HEADS, GDN_DV).astype(jnp.float32)
    o = rms_norm(o, norm_w) * jax.nn.silu(z)
    return o.reshape(bsz, t_, GDN_V_WIDTH).astype(q_raw.dtype), s_fin, new_buf

def mixer(h, w_in_l, fox_f_bias_l, fox_norm_w_l, gdn_conv_w_l, gdn_a_log_l, gdn_dt_bias_l, gdn_norm_w_l,
          w_out_l, fox_cache, conv_buf, s0):
    bsz, t_ = h.shape[:2]
    proj = h @ w_in_l
    parts = []
    start = 0
    for width in IN_SPLITS:
        parts.append(proj[..., start:start + width])
        start += width
    fq, fk, fv, ff, gq, gk, gv, ga, gb, gz = parts
    fq = fq.reshape(bsz, t_, FOX_HEADS, HEAD_DIM)
    fk = fk.reshape(bsz, t_, FOX_HEADS, HEAD_DIM)
    fv = fv.reshape(bsz, t_, FOX_HEADS, HEAD_DIM)
    logf = jax.nn.log_sigmoid(ff.astype(jnp.float32) + fox_f_bias_l.astype(jnp.float32))
    if fox_cache is None:
        fo = fox_prompt(fq, fk, fv, logf)
    else:
        fo = fox_sample(fq, fk, fv, logf, fox_cache[0], fox_cache[1], fox_cache[2])
    fo = rms_norm(fo, fox_norm_w_l).reshape(bsz, t_, FOX_WIDTH)
    go, s_fin, new_buf = gdn_mixer(gq, gk, gv, ga, gb, gz, conv_buf, s0,
                                   gdn_conv_w_l, gdn_a_log_l, gdn_dt_bias_l, gdn_norm_w_l)
    out = jnp.concatenate([fo, go.astype(fo.dtype)], axis=-1) @ w_out_l
    return out, (fk, fv, logf, s_fin, new_buf)

def swiglu(x, w_gate, w_up, w_down):
    return (jax.nn.silu(x @ w_gate) * (x @ w_up)) @ w_down

def setup_inputs(seed: int = 0) -> dict:
    key = jax.random.key(seed)
    ks = jax.random.split(key, 32)
    f32 = jnp.float32

    def nrm(k, shape, scale):
        return jax.random.normal(k, shape, f32) * scale

    dt = jnp.exp(jax.random.uniform(ks[14], (DEPTH, GDN_HEADS), f32, math.log(DT_MIN), math.log(DT_MAX)))
    return {
        'x_prompt': nrm(ks[0], (BATCH, SEQ, D_MODEL), 1.0),
        'x_sample': nrm(ks[1], (DEC_BATCH, DEC_SEQ, D_MODEL), 1.0),
        'cache_fox_k': nrm(ks[2], (DEPTH, DEC_BATCH, PAST_LEN, FOX_HEADS, HEAD_DIM), 1.0),
        'cache_fox_v': nrm(ks[3], (DEPTH, DEC_BATCH, PAST_LEN, FOX_HEADS, HEAD_DIM), 1.0),
        'cache_fox_logf': jax.nn.log_sigmoid(nrm(ks[4], (DEPTH, DEC_BATCH, PAST_LEN, FOX_HEADS), 1.0)
                                             + FGATE_BIAS_MEAN),
        'state_gdn': nrm(ks[5], (DEPTH, DEC_BATCH, GDN_HEADS, GDN_DK, GDN_DV), 0.1),
        'state_gdn_conv': nrm(ks[6], (DEPTH, DEC_BATCH, CONV_W - 1, GDN_CONV_CH), 1.0),
        'ln_in_g': 1.0 + nrm(ks[7], (D_MODEL,), 0.05),
        'ln_in_b': nrm(ks[8], (D_MODEL,), 0.02),
        'w_in': nrm(ks[9], (DEPTH, D_MODEL, IN_COLS), D_MODEL ** -0.5),
        'fox_f_bias': FGATE_BIAS_MEAN + nrm(ks[10], (DEPTH, FOX_HEADS), 0.1),
        'fox_norm_w': 1.0 + nrm(ks[11], (DEPTH, HEAD_DIM), 0.05),
        'gdn_conv_w': nrm(ks[12], (DEPTH, CONV_W, GDN_CONV_CH), CONV_W ** -0.5),
        'gdn_a_log': jnp.log(jax.random.uniform(ks[13], (DEPTH, GDN_HEADS), f32, 1.0, 16.0)),
        'gdn_dt_bias': dt + jnp.log(-jnp.expm1(-dt)),
        'gdn_norm_w': 1.0 + nrm(ks[15], (DEPTH, GDN_DV), 0.05),
        'w_out': nrm(ks[16], (DEPTH, MIX_WIDTH, D_MODEL), MIX_WIDTH ** -0.5 * DEEPNORM_BETA),
        'ln_mix_g': 1.0 + nrm(ks[17], (DEPTH, D_MODEL), 0.05),
        'ln_mix_b': nrm(ks[18], (DEPTH, D_MODEL), 0.02),
        'ffn_w_gate': nrm(ks[19], (DEPTH, D_MODEL, D_FF), D_MODEL ** -0.5),
        'ffn_w_up': nrm(ks[20], (DEPTH, D_MODEL, D_FF), D_MODEL ** -0.5),
        'ffn_w_down': nrm(ks[21], (DEPTH, D_FF, D_MODEL), D_FF ** -0.5 * DEEPNORM_BETA),
        'ln_ffn_g': 1.0 + nrm(ks[22], (DEPTH, D_MODEL), 0.05),
        'ln_ffn_b': nrm(ks[23], (DEPTH, D_MODEL), 0.02),
    }

def reference(x_prompt, x_sample, cache_fox_k, cache_fox_v, cache_fox_logf, state_gdn, state_gdn_conv,
              ln_in_g, ln_in_b, w_in, fox_f_bias, fox_norm_w, gdn_conv_w, gdn_a_log, gdn_dt_bias, gdn_norm_w,
              w_out, ln_mix_g, ln_mix_b, ffn_w_gate, ffn_w_up, ffn_w_down, ln_ffn_g, ln_ffn_b):
    xp = layer_norm(x_prompt, ln_in_g, ln_in_b)
    xs = layer_norm(x_sample, ln_in_g, ln_in_b)
    ps = []
    ss = []
    for l in range(DEPTH):
        lw = (w_in[l], fox_f_bias[l], fox_norm_w[l], gdn_conv_w[l], gdn_a_log[l], gdn_dt_bias[l],
              gdn_norm_w[l], w_out[l])
        bp = xp.shape[0]
        mp, st_p = mixer(xp, *lw, None,
                         jnp.zeros((bp, CONV_W - 1, GDN_CONV_CH), xp.dtype),
                         jnp.zeros((bp, GDN_HEADS, GDN_DK, GDN_DV), jnp.float32))
        ms, st_s = mixer(xs, *lw, (cache_fox_k[l], cache_fox_v[l], cache_fox_logf[l]),
                         state_gdn_conv[l], state_gdn[l])
        xp = layer_norm(DEEPNORM_ALPHA * xp + mp, ln_mix_g[l], ln_mix_b[l])
        xs = layer_norm(DEEPNORM_ALPHA * xs + ms, ln_mix_g[l], ln_mix_b[l])
        xp = layer_norm(DEEPNORM_ALPHA * xp + swiglu(xp, ffn_w_gate[l], ffn_w_up[l], ffn_w_down[l]),
                        ln_ffn_g[l], ln_ffn_b[l])
        xs = layer_norm(DEEPNORM_ALPHA * xs + swiglu(xs, ffn_w_gate[l], ffn_w_up[l], ffn_w_down[l]),
                        ln_ffn_g[l], ln_ffn_b[l])
        ps.append(st_p)
        ss.append(st_s)

    def stacked(states, i):
        return jnp.stack([st[i] for st in states], axis=0)

    return (xp, xs,
            stacked(ps, 0), stacked(ps, 1), stacked(ps, 2), stacked(ps, 3), stacked(ps, 4),
            stacked(ss, 0), stacked(ss, 1), stacked(ss, 2), stacked(ss, 3), stacked(ss, 4))


_drawn_inputs = setup_inputs


def setup_inputs(seed=0):
    import zlib

    import numpy as np

    out = dict(_drawn_inputs(seed))
    spreads = {}
    factors = {'fox_norm_w': 3.056, 'gdn_norm_w': 5.906, 'ln_mix_b': 2.726, 'ln_ffn_b': 2.881}
    for name, (base, spread) in spreads.items():
        noise = np.random.default_rng([zlib.crc32(name.encode()), seed]).standard_normal(out[name].shape)
        drawn = base * np.exp(spread * noise) if base else spread * noise
        out[name] = __import__('jax').numpy.asarray(drawn.astype(out[name].dtype))
    for name, factor in factors.items():
        out[name] = (out[name] * factor).astype(out[name].dtype)
    return out
```

```python
from contextlib import ExitStack

import numpy as np

import concourse.bass as bass
from concourse import mybir

F32 = mybir.dt.float32
F32R = mybir.dt.float32r
ALU = mybir.AluOpType
ACT = mybir.ActivationFunctionType
AX = mybir.AxisListType.X

P = 128
D = 2048
TT = 3
TOK = TT * P
HEADS = 8
HD = 128
NB = 8
NQ = 16
DFF = 5632
KD = D // P
CW = 512
KP = 2
RAW = 4
RING = 2
SEG = TOK // NQ
TAP = 4
ALPHA = 2.0 ** 0.25
NEG = -1.0e30
SCALE = HD ** -0.5

FQ, FK, FV, FF = 0, 1024, 2048, 3072
GQ, GA, GZ = 3080, 6152, 6168

NP_IN = KD // KP
G_FOX = 0
G_GDN = G_FOX + HEADS * NP_IN
G_OUT_FOX = G_GDN + HEADS * NP_IN
NCB = D // CW
NP_HALF = NP_IN // 2
G_OUT_GDN = G_OUT_FOX + NCB * NP_HALF
G_UP0 = G_OUT_GDN + NCB * NP_HALF
FB = (6, 5)
KH = FB[0] * CW // P
NP_DN = (FB[0] * CW // P // KP, FB[1] * CW // P // KP)
G_DN0 = G_UP0 + FB[0] * 2 * NP_IN
G_UP1 = G_DN0 + NCB * NP_DN[0]
G_DN1 = G_UP1 + FB[1] * 2 * NP_IN
G_END = G_DN1 + NCB * NP_DN[1]

C_ID, C_ONE, C_LP, C_LS, C_UP, C_US = (P * n for n in range(6))
C_MP = 6 * P
C_MS = C_MP + 2 * P
C_LV = C_MS + 2 * P
LEVELS = 7
F_OWN = 6
G_OWN = 20
C_BM = C_LV + LEVELS * P
NC = C_BM + NB


def constants():
    i = np.arange(P)
    row, col = i[:, None], i[None, :]
    same = row // NQ == col // NQ
    c = np.zeros((P, NC), np.float32)
    c[:, C_ID:C_ID + P] = row == col
    c[:, C_ONE:C_ONE + P] = 1
    c[:, C_LP:C_LP + P] = row <= col
    c[:, C_LS:C_LS + P] = (row <= col) & same
    c[:, C_UP:C_UP + P] = row > col
    c[:, C_US:C_US + P] = (row > col) & same
    c[:, C_MP + P:C_MP + 2 * P] = np.where(col <= row, 0, NEG)
    c[:, C_MS + P:C_MS + 2 * P] = np.where((col <= row) & same, 0, NEG)
    for n in range(LEVELS):
        s = 1 << n
        c[:, C_LV + n * P:C_LV + (n + 1) * P] = (row // (2 * s) == col // (2 * s)) & (row // s % 2 == 1) & (col // s % 2 == 0)
    c[:, C_BM:C_BM + NB] = row // NQ == np.arange(NB)[None, :]
    return c


class Course:

    def __init__(self, program):
        self.program, self.at = program, next(program)

    def upto(self, n):
        while self.at is not None and (n is None or self.at <= n):
            self.at = next(self.program, None)


def encoder_layer(nc, x_prompt, x_sample, cache_k, cache_v, cache_logf, state_gdn, state_conv, ln_in_g, ln_in_b,
                  w_in, fox_f_bias, fox_norm_w, gdn_conv_w, gdn_a_log, gdn_dt_bias, gdn_norm_w, w_out, ln_mix_g,
                  ln_mix_b, w_gate, w_up, w_down, ln_ffn_g, ln_ffn_b, const_in,
                  y_prompt, y_sample, o_kp, o_vp, o_lfp, o_sp, o_cp, o_ks, o_vs, o_lfs, o_ss, o_cs):
    w_in, w_out, w_gate, w_up, w_down = w_in[0], w_out[0], w_gate[0], w_up[0], w_down[0]
    sems = {}
    top = ExitStack()

    def sem(name):
        if name not in sems:
            sems[name] = top.enter_context(nc.semaphore(name))
        return sems[name]

    def pool_wait(pool, event, value):
        pool.wait_ge(event, value)
        pool.sem_inc(sem("pool_waited"), 1)

    def sb(ctx, name, shape, dt=F32):
        return ctx.enter_context(nc.sbuf_tensor(name, shape, dt))

    with top:
        x_res = sb(top, "x_res", [P, TT, D])
        aT_hi = sb(top, "aT_hi", [P, KD, TOK], F32R)
        aT_lo = sb(top, "aT_lo", [P, KD, TOK], F32R)
        raw = sb(top, "raw", [P, RAW, KP, CW])
        w_hi = sb(top, "w_hi", [P, RING, KP, CW], F32R)
        w_lo = sb(top, "w_lo", [P, RING, KP, CW], F32R)
        cn = sb(top, "cn", [P, NC])
        bank = [top.enter_context(nc.psum_tensor(f"bank{n}", [P, 512], F32)) for n in range(8)]
        ident, ones = cn[:, C_ID:C_ID + P], cn[:, C_ONE:C_ONE + P]
        stats = sb(top, "stats", [P, TT, D // 512, 6])
        moments = sb(top, "moments", [P, TT, 2])
        rstd = sb(top, "rstd", [P, TT])
        var = sb(top, "var", [P, TT])
        pol = sb(top, "pol", [P, TT])
        ACC, ACC2 = bank[0:3], bank[3:6]

        def loads(sp, g, slot, parts, first=False):
            if not first:
                sp.wait_ge(sem("w_split"), g - RAW + 1)
            for dst, src in parts:
                sp.dma_start(dst, src).then_inc(sem(f"w_loaded{slot}"), 16)

        def dmas_of(g):
            return 3 if g < G_OUT_FOX + RING else 2

        def plain_parts(w, row, c0, slot, dmas=2):
            parts = [(raw[:, slot, k, :], w[bass.ds(row + k * P, P), bass.ds(c0, CW)]) for k in range(KP)]
            if dmas == 3:
                half = CW // 2
                parts[1:] = [(raw[:, slot, 1, c:c + half], w[bass.ds(row + P, P), bass.ds(c0 + c, half)])
                             for c in (0, half)]
            return parts

        def head_columns(row, c0, h):
            return w_in[row:row + KP * P, c0:c0 + HEADS * HD].rearrange("(k p) (h c) -> p k h c", p=P, c=HD)[:, :, h, :]

        def fox_parts(h, n, slot):
            return [(raw[:, slot, :, a * HD:(a + 1) * HD], head_columns(n * KP * P, c0, h))
                    for a, c0 in enumerate((FQ, FK, FV))]

        def gdn_parts(h, n, slot):
            qkv = w_in[n * KP * P:(n + 1) * KP * P, GQ:GA].rearrange("(k p) (a h c) -> p k a h c", p=P, a=3, c=HD)
            return [(raw[:, slot, k, 0:3 * HD].rearrange("p (a c) -> p a c", a=3), qkv[:, k, :, h, :])
                    for k in range(KP)] + [(raw[:, slot, :, 3 * HD:], head_columns(n * KP * P, GZ, h))]

        def landed(g0, n, i, per):
            def total(g):
                return 16 * sum(dmas_of(q) for q in range(g % RAW, g + 1, RAW))
            first = total(g0 + n)
            return first + (total(g0 + n + per) - first) * i if per else first

        def split_act(act, g0, n, i=0, per=0):
            g = g0 + n
            act.wait_ge(sem(f"w_loaded{g % RAW}"), landed(g0, n, i, per))
            if g >= RING:
                act.wait_ge(sem("w_used"), g + per * i - RING + 1)
            nc.scalar.activation(w_hi[:, g % RING], raw[:, g % RAW], ACT.Copy).then_inc(sem("w_high"), 1)

        def split_dve(dve, g0, n, i=0, per=0):
            g = g0 + n
            dve.wait_ge(sem("w_high"), g + per * i + 1)
            nc.vector.tensor_tensor(w_lo[:, g % RING], raw[:, g % RAW], w_hi[:, g % RING],
                                    ALU.subtract).then_inc(sem("w_split"), 1)

        def gemm(pe, g0, pieces, hi, lo, k0, width, acc, name, block, i=0, per=0, blocks_per=0, between=None,
                 first=False, ends=True):
            for n in range(pieces):
                g = g0 + n
                pe.wait_ge(sem("w_split"), g + per * i + 1)
                for t in range(TT):
                    if n == 0 and not first:
                        pe.wait_ge(sem(name + "_free"), TT * (block - 1 + blocks_per * i) + t + 1)
                    for k in range(KP):
                        kt = k0 + n * KP + k
                        for j, (l, r) in enumerate(((hi, w_hi), (hi, w_lo), (lo, w_hi))):
                            last = nc.tensor.matmul(acc[t][:, 0:width], l[:, kt, t * P:(t + 1) * P],
                                                    r[:, g % RING, k, 0:width],
                                                    start=(n == 0 and k == 0 and j == 0),
                                                    stop=(n == pieces - 1 and k == KP - 1 and j == 2))
                    if t == TT - 1:
                        last.then_inc(sem("w_used"), 1)
                    elif n == pieces - 1:
                        last.then_inc(sem(name + "_done"), 1)
                    if between is not None:
                        next(between, None)
            if between is not None and ends:
                for _ in between:
                    pass

        def wait_acc(eng, name, block, t, g_end):
            if t < TT - 1:
                eng.wait_ge(sem(name + "_done"), (TT - 1) * block + t + 1)
            else:
                eng.wait_ge(sem("w_used"), g_end)

        def rsqrt_act(act, y, x, ln_sem, ln_count, done):
            nc.scalar.activation(y, x, ACT.Ln).then_inc(sem(ln_sem), 1)
            act.wait_ge(sem(ln_sem), ln_count)
            nc.scalar.activation(y, y, ACT.Exp, scale=-0.5).then_inc(sem(done), 1)

        def polish(y, x, tmp, after):
            after(nc.vector.tensor_tensor(tmp, y, y, ALU.mult))
            after(nc.vector.scalar_tensor_tensor(out=tmp, in0=tmp, scalar=-0.5, in1=x, op0=ALU.mult, op1=ALU.mult))
            after(nc.vector.scalar_tensor_tensor(out=y, in0=tmp, scalar=1.5, in1=y, op0=ALU.add, op1=ALU.mult))

        chain = [0]

        def link(dve, ins):
            chain[0] += 1
            ins.then_inc(sem("dve_chain"), 1)
            dve.wait_ge(sem("dve_chain"), chain[0])

        def layer_norm_act(act, t, norm):
            act.wait_ge(sem("ln_var"), TT * norm + t + 1)
            rsqrt_act(act, rstd[:, t:t + 1], var[:, t:t + 1], "ln_ln", TT * norm + t + 1, "ln_rstd")

        def layer_norm_dve(dve, t, gb, norm):
            for q in range(D // 512):
                last = nc.vector.bn_stats(stats[:, t, q, :], x_res[:, t, q * 512:(q + 1) * 512])
            link(dve, last)
            link(dve, nc.vector.bn_aggr(moments[:, t, :], stats[:, t].rearrange("p a b -> p (a b)")))
            nc.vector.tensor_scalar(var[:, t:t + 1], moments[:, t, 1:2], 1e-5, None, ALU.add)\
                .then_inc(sem("ln_var"), 1)
            dve.wait_ge(sem("ln_rstd"), TT * norm + t + 1)
            polish(rstd[:, t:t + 1], var[:, t:t + 1], pol[:, 0:1], lambda ins: link(dve, ins))
            link(dve, nc.vector.tensor_scalar(x_res[:, t, :], x_res[:, t, :], moments[:, t, 0:1], rstd[:, t:t + 1],
                                              ALU.subtract, ALU.mult))
            if t == 0:
                dve.wait_ge(sem("gb_in"), 32 * (norm + 1))
            link(dve, nc.vector.tensor_tensor(x_res[:, t, :], x_res[:, t, :], gb[:, 0, :], ALU.mult))
            link(dve, nc.vector.tensor_tensor(x_res[:, t, :], x_res[:, t, :], gb[:, 1, :], ALU.add))
            dve.sem_inc(sem("ln_done"), 1)

        def load_gb(eng, gb, g, b):
            eng.dma_start(gb[:, 0, :], g.partition_broadcast(P)).then_inc(sem("gb_in"), 16)
            eng.dma_start(gb[:, 1, :], b.partition_broadcast(P)).then_inc(sem("gb_in"), 16)

        ROUNDS = TT * KD // 4

        def x_transpose_pe(pe, r, norm):
            t, k4 = divmod(r, KD // 4)
            if k4 == 0:
                pe.wait_ge(sem("ln_done"), TT * norm + t + 1)
            if r >= 2:
                pe.wait_ge(sem("x_low"), ROUNDS * norm + r - 1)
            for k in range(4):
                c = (k4 * 4 + k) * P
                last = nc.tensor.transpose(bank[6 + r % 2][:, k * P:(k + 1) * P], x_res[:, t, c:c + P], ident)
            last.then_inc(sem("x_ps"), 1)

        def x_evac(r, dst):
            t, k4 = divmod(r, KD // 4)
            return (dst[:, 4 * k4:4 * k4 + 4, t * P:(t + 1) * P],
                    bank[6 + r % 2][:, :].rearrange("p (k c) -> p k c", k=4))

        def x_evac_act(act, r, norm):
            act.wait_ge(sem("x_ps"), ROUNDS * norm + r + 1)
            dst, src = x_evac(r, aT_hi)
            nc.scalar.activation(dst, src, ACT.Copy).then_inc(sem("x_high"), 1)

        def x_evac_dve(dve, r, norm):
            dve.wait_ge(sem("x_high"), ROUNDS * norm + r + 1)
            lo, src = x_evac(r, aT_lo)
            nc.vector.tensor_tensor(lo, src, x_evac(r, aT_hi)[0], ALU.subtract).then_inc(sem("x_low"), 1)

        mid = ExitStack()
        with mid:
            mixT_hi = sb(mid, "mixT_hi", [P, 2 * HEADS, TOK], F32R)
            mixT_lo = sb(mid, "mixT_lo", [P, 2 * HEADS, TOK], F32R)
            gate = sb(mid, "gate", [P, TT, 24])
            cfox = sb(mid, "cfox", [P, TT, HEADS])
            ccache = sb(mid, "ccache", [P, NB, HEADS])
            ncT = sb(mid, "ncT", [HEADS, TOK])
            nGT = sb(mid, "nGT", [HEADS, TOK])
            Gc = sb(mid, "Gc", [P, TT, HEADS])
            eG = sb(mid, "eG", [P, TT, HEADS])
            eR = sb(mid, "eR", [P, TT, HEADS])
            eL = sb(mid, "eL", [P, 2 + NB, HEADS])
            beta = sb(mid, "beta", [P, TT, HEADS])
            bhalf = sb(mid, "bhalf", [P, TT, HEADS])
            nbe = sb(mid, "nbe", [P, TT, HEADS])
            cw = sb(mid, "cw", [P, TAP * 24])
            cprev = sb(mid, "cprev", [P, 24, NB * 3])
            nwf = sb(mid, "nwf", [P, 1])
            nwg = sb(mid, "nwg", [P, 1])
            nwg2 = sb(mid, "nwg2", [P, 1])
            gbuf = sb(mid, "gbuf", [P, TT, CW])

            with ExitStack() as ctx:
                gb = sb(ctx, "gb0", [P, 2, D])
                wg = sb(ctx, "wg", [P, KD, 24])
                wg_hi = sb(ctx, "wg_hi", [P, KD, 24], F32R)
                wg_lo = sb(ctx, "wg_lo", [P, KD, 24], F32R)
                gT = sb(ctx, "gT", [24, TOK])
                gbias = sb(ctx, "gbias", [P, 24])
                alog = sb(ctx, "alog", [P, HEADS])
                ea = sb(ctx, "ea", [P, HEADS])
                mag = sb(ctx, "mag", [P, TT, 16])
                soft = sb(ctx, "soft", [P, TT, 16])
                lf = sb(ctx, "lf", [P, TT, HEADS])
                gl = sb(ctx, "gl", [P, TT, HEADS])
                glb = sb(ctx, "glb", [P, NB, HEADS])
                lc = sb(ctx, "lc", [P, NB, HEADS])
                tsel = sb(ctx, "tsel", [P, NB, HEADS])
                tsum = sb(ctx, "tsum", [P, HEADS])
                cwraw = sb(ctx, "cwraw", [TAP * 24, P])
                stc = sb(ctx, "stc", [2 * NB * 3, 12 * P])
                SB_ = bank[5]
                S_C, S_G, S_R, S_TP, S_TS, S_CC, S_CT = 0, 24, 48, 72, 88, 152, 216
                block = ctx.enter_context(nc.Block())

                @block.sync
                def _(sp):
                    sp.dma_start(x_res[:, 0, :], x_prompt[0, 0:P, :]).then_inc(sem("x_in0"), 16)
                    sp.dma_start(x_res[:, 1, :], x_prompt[0, P:2 * P, :]).then_inc(sem("x_in1"), 16)
                    sp.dma_start(x_res[:, 2, :], x_sample.rearrange("b s d -> (b s) d")).then_inc(sem("x_in2"), 16)
                    load_gb(sp, gb, ln_in_g, ln_in_b)
                    for n in range(RAW):
                        sp.wait_ge(sem("raw_zero"), 1)
                        loads(sp, n, n, fox_parts(0, n, n), first=True)
                    for n in range(RAW, RAW + RING):
                        loads(sp, n, n % RAW, fox_parts(0, n, n % RAW))

                @block.gpsimd
                def _(pool):
                    pool.dma_start(cn[:], const_in).then_inc(sem("consts"), 16)
                    pool.dma_start(wg[:, :, 0:8], w_in[:, FF:FF + 8].rearrange("(k p) c -> p k c", p=P))\
                        .then_inc(sem("small"), 16)
                    pool.dma_start(wg[:, :, 8:24], w_in[:, GA:GZ].rearrange("(k p) c -> p k c", p=P))\
                        .then_inc(sem("small"), 16)
                    nc.gpsimd.memset(gbias[:], 0.0).then_inc(sem("bias_zero"), 1)
                    pool_wait(pool, sem("bias_zero"), 1)
                    pool.dma_start(gbias[:, 0:8], fox_f_bias[0].partition_broadcast(P)).then_inc(sem("small"), 16)
                    pool.dma_start(gbias[:, 8:16], gdn_dt_bias[0].partition_broadcast(P)).then_inc(sem("small"), 16)
                    pool.dma_start(alog[:], gdn_a_log[0].partition_broadcast(P)).then_inc(sem("small"), 16)
                    pool.dma_start(lc[:], cache_logf[0].rearrange("b t h -> t b h")).then_inc(sem("small"), 16)
                    pool.dma_start(nwf[:], fox_norm_w.rearrange("a p -> p a")).then_inc(sem("small"), 16)
                    pool.dma_start(nwg[:], gdn_norm_w.rearrange("a p -> p a")).then_inc(sem("small"), 16)
                    pool.dma_start(cwraw[:], gdn_conv_w[0].rearrange("r (c p) -> (r c) p", p=P))\
                        .then_inc(sem("small"), 16)
                    for half in range(2):
                        pool.dma_start(stc[half * 24:half * 24 + 24, :],
                                       state_conv[0].rearrange("b r c -> (b r) c")[:, half * 12 * P:(half + 1) * 12 * P])\
                            .then_inc(sem("small"), 16)
                    pool_wait(pool, sem("lf_ready"), 1)
                    pool.dma_start(o_lfp[0, 0].rearrange("(t p) h -> p t h", p=P), lf[:, 0:2, :])\
                        .then_inc(sem("lf_stored"), 16)
                    pool.dma_start(o_lfs[0].rearrange("b s h -> (b s) h"), lf[:, 2, :])\
                        .then_inc(sem("lf_stored"), 16)
                    pool_wait(pool, sem("lf_stored"), 32)

                @block.scalar
                def _(act):
                    act.wait_ge(sem("small"), 16 * 11)
                    nc.scalar.activation(wg_hi[:], wg[:], ACT.Copy).then_inc(sem("wg_high"), 1)
                    nc.scalar.activation(ea[:], alog[:], ACT.Exp).then_inc(sem("ea"), 1)
                    for n in range(RING):
                        split_act(act, n, 0)
                    for r in range(ROUNDS):
                        if r % (ROUNDS // TT) == 0:
                            layer_norm_act(act, r // (ROUNDS // TT), 0)
                        x_evac_act(act, r, 0)
                    act.wait_ge(sem("g_ps"), 1)
                    nc.scalar.activation(gT[:], bank[3][0:24, 0:TOK], ACT.Copy).then_inc(sem("gT"), 1)
                    act.wait_ge(sem("mag"), 1)
                    nc.scalar.activation(mag[:], mag[:], ACT.Exp, scale=-1.0).then_inc(sem("emag"), 1)
                    act.wait_ge(sem("emag"), 1)
                    nc.scalar.activation(mag[:], mag[:], ACT.Ln, bias=1.0).then_inc(sem("lnmag"), 1)
                    nc.scalar.activation(beta[:], gate[:, :, 16:24], ACT.Tanh, scale=0.5).then_inc(sem("tanhb"), 1)
                    act.wait_ge(sem("sums"), 1)
                    nc.scalar.activation(eG[:], SB_[:, S_G:S_G + 24].rearrange("p (t h) -> p t h", t=TT), ACT.Exp)
                    nc.scalar.activation(eR[:], SB_[:, S_R:S_R + 24].rearrange("p (t h) -> p t h", t=TT), ACT.Exp)
                    nc.scalar.activation(eL[:], SB_[:, S_TP:S_CC].rearrange("p (t h) -> p t h", h=HEADS), ACT.Exp)\
                        .then_inc(sem("exps"), 1)

                @block.vector
                def _(dve):
                    nc.vector.memset(raw[:], 0.0).then_inc(sem("raw_zero"), 1)
                    for t in range(TT):
                        dve.wait_ge(sem(f"x_in{t}"), 16)
                        layer_norm_dve(dve, t, gb, 0)
                        if t == 0:
                            for n in range(RING):
                                split_dve(dve, n, 0)
                        for r in range(t * 4, t * 4 + 4):
                            x_evac_dve(dve, r, 0)
                    dve.wait_ge(sem("wg_high"), 1)
                    nc.vector.tensor_tensor(wg_lo[:], wg[:], wg_hi[:], ALU.subtract).then_inc(sem("wg_low"), 1)
                    dve.wait_ge(sem("gate_ps"), 1)
                    bias = gbias[:].unsqueeze(1).broadcast_to([P, TT, 24])
                    link(dve, nc.vector.tensor_tensor(
                        gate[:], bank[4][:, 0:72].rearrange("p (t c) -> p t c", t=TT), bias, ALU.add))
                    link(dve, nc.vector.tensor_scalar(gate[:, :, 0:8], gate[:, :, 0:8], -1.0, None, ALU.mult))
                    nc.vector.scalar_tensor_tensor(out=mag[:], in0=gate[:, :, 0:16], scalar=-1.0,
                                                   in1=gate[:, :, 0:16], op0=ALU.mult, op1=ALU.max)\
                        .then_inc(sem("mag"), 1)
                    dve.wait_ge(sem("lnmag"), 1)
                    link(dve, nc.vector.scalar_tensor_tensor(out=soft[:], in0=gate[:, :, 0:16], scalar=0.0,
                                                             in1=mag[:], op0=ALU.max, op1=ALU.add))
                    nc.vector.tensor_scalar(lf[:], soft[:, :, 0:8], -1.0, None, ALU.mult).then_inc(sem("lf_ready"), 1)
                    dve.wait_ge(sem("ea"), 1)
                    link(dve, nc.vector.scalar_tensor_tensor(
                        out=gl[:], in0=soft[:, :, 8:16], scalar=-1.0,
                        in1=ea[:].unsqueeze(1).broadcast_to([P, TT, HEADS]), op0=ALU.mult, op1=ALU.mult))
                    nc.vector.tensor_tensor(
                        glb[:], gl[:, 2, :].unsqueeze(1).broadcast_to([P, NB, HEADS]),
                        cn[:, C_BM:C_BM + NB].unsqueeze(2).broadcast_to([P, NB, HEADS]), ALU.mult)\
                        .then_inc(sem("gl_ready"), 1)
                    dve.wait_ge(sem("tanhb"), 1)
                    link(dve, nc.vector.tensor_scalar(beta[:], beta[:], 1.0, 0.5, ALU.add, ALU.mult))
                    nc.vector.tensor_scalar(bhalf[:], beta[:], 0.5, None, ALU.mult)
                    link(dve, nc.vector.tensor_scalar(nwg2[:], nwg[:], 0.5, None, ALU.mult))
                    dve.wait_ge(sem("exps"), 1)
                    link(dve, nc.vector.scalar_tensor_tensor(out=nbe[:], in0=beta[:], scalar=-1.0, in1=eG[:],
                                                             op0=ALU.mult, op1=ALU.mult))
                    link(dve, nc.vector.tensor_tensor(
                        tsel[:], SB_[:, S_CT:S_CT + 64].rearrange("p (b h) -> p b h", b=NB),
                        cn[:, C_BM:C_BM + NB].unsqueeze(2).broadcast_to([P, NB, HEADS]), ALU.mult))
                    nc.vector.tensor_copy(cfox[:, 0:2, :], SB_[:, S_C:S_C + 16].rearrange("p (t h) -> p t h", t=2))
                    nc.vector.tensor_copy(Gc[:], SB_[:, S_G:S_G + 24].rearrange("p (t h) -> p t h", t=TT))
                    nc.vector.tensor_copy(ccache[:], SB_[:, S_CC:S_CC + 64].rearrange("p (b h) -> p b h", b=NB))
                    link(dve, nc.vector.tensor_reduce(tsum[:], tsel[:].rearrange("p b h -> p h b"), AX, ALU.add))
                    nc.vector.tensor_tensor(cfox[:, 2, :], SB_[:, S_C + 16:S_C + 24], tsum[:], ALU.add)\
                        .then_inc(sem("c_ready"), 1)
                    dve.wait_ge(sem("cT_ps"), 1)
                    nc.vector.tensor_scalar(ncT[:], bank[6][0:HEADS, 0:TOK], -1.0, None, ALU.mult)
                    nc.vector.tensor_scalar(nGT[:], bank[7][0:HEADS, 0:TOK], -1.0, None, ALU.mult)
                    nc.vector.tensor_copy(cw[:], bank[4][:, 128:128 + TAP * 24])
                    for j in range(2):
                        nc.vector.tensor_copy(
                            cprev[:].rearrange("p (g c) r -> p c g r", g=2)[:, 6 * j:6 * j + 6],
                            bank[j][:, 0:288].rearrange("p (c g r) -> p c g r", c=6, g=2))
                    nc.vector.drain().then_inc(sem("start_done"), 1)

                @block.tensor
                def _(pe):
                    pe.wait_ge(sem("consts"), 16)
                    for r in range(ROUNDS):
                        x_transpose_pe(pe, r, 0)
                    pe.wait_ge(sem("wg_low"), 1)
                    for k in range(KD):
                        for j, (w, x) in enumerate(((wg_hi, aT_hi), (wg_hi, aT_lo), (wg_lo, aT_hi))):
                            last = nc.tensor.matmul(bank[3][0:24, 0:TOK], w[:, k, :], x[:, k, :],
                                                    start=(k == 0 and j == 0), stop=(k == KD - 1 and j == 2))
                    last.then_inc(sem("g_ps"), 1)
                    pe.wait_ge(sem("gT"), 1)
                    for t in range(TT):
                        last = nc.tensor.transpose(bank[4][:, t * 24:t * 24 + 24], gT[:, t * P:(t + 1) * P],
                                                   ident[0:24, 0:24])
                    last.then_inc(sem("gate_ps"), 1)
                    for c in range(12):
                        nc.tensor.transpose(bank[c // 6][:, c % 6 * 48:c % 6 * 48 + 48], stc[:, c * P:(c + 1) * P],
                                            ident[0:48, 0:48])
                    pe.wait_ge(sem("gl_ready"), 1)
                    LP, LS = cn[:, C_LP:C_LP + P], cn[:, C_LS:C_LS + P]
                    UP, US = cn[:, C_UP:C_UP + P], cn[:, C_US:C_US + P]

                    def sums(col, pairs):
                        for j, (l, r) in enumerate(pairs):
                            ins = nc.tensor.matmul(SB_[:, col:col + r.free_size()], l, r,
                                                   start=(j == 0), stop=(j == len(pairs) - 1))
                        return ins
                    sums(S_C, [(LP, lf[:, 0, :])])
                    sums(S_C + 8, [(LP, lf[:, 1, :]), (ones, lf[:, 0, :])])
                    sums(S_C + 16, [(LS, lf[:, 2, :])])
                    for t in range(TT):
                        sums(S_G + 8 * t, [(LP if t < 2 else LS, gl[:, t, :])])
                        sums(S_R + 8 * t, [(UP if t < 2 else US, gl[:, t, :])])
                    for t in range(2):
                        sums(S_TP + 8 * t, [(ones, gl[:, t, :])])
                    sums(S_TS, [(ones, glb[:].rearrange("p b h -> p (b h)"))])
                    sums(S_CC, [(LP, lc[:].rearrange("p b h -> p (b h)"))])
                    sums(S_CT, [(ones, lc[:].rearrange("p b h -> p (b h)"))]).then_inc(sem("sums"), 1)
                    nc.tensor.transpose(bank[4][:, 128:128 + TAP * 24], cwraw[:], ident[0:TAP * 24, 0:TAP * 24])
                    pe.wait_ge(sem("c_ready"), 1)
                    for t in range(TT):
                        nc.tensor.transpose(bank[6][0:HEADS, t * P:(t + 1) * P], cfox[:, t, :], ident)
                        last = nc.tensor.transpose(bank[7][0:HEADS, t * P:(t + 1) * P], Gc[:, t, :], ident)
                    last.then_inc(sem("cT_ps"), 1)

            b3, b4, b5, b6, b7 = bank[3:8]

            def tiles(ap, n=TT):
                return ap.rearrange("p (t c) -> p t c", t=n)

            def per_token(x, h, n=TT):
                return x[:, 0:n, bass.ds(h, 1)].broadcast_to([P, n, HD])

            with ExitStack() as ctx:
                fbuf = sb(ctx, "fbuf", [P, TT, 3 * HD])
                kc = sb(ctx, "kc", [P, NB, HD])
                vc = sb(ctx, "vc", [P, NB, HD])
                qkT = sb(ctx, "f_qkT", [P, 2, TOK])
                kcT = sb(ctx, "kcT", [P, NB * HD])
                nch = sb(ctx, "nch", [HEADS, TOK])
                scT = sb(ctx, "scT", [P, P])
                sc = sb(ctx, "sc", [P, TT, 2 * P])
                nmax = sb(ctx, "nmax", [P, TT])
                den = sb(ctx, "den", [P, TT])
                rden = sb(ctx, "rden", [P, TT])
                pT = sb(ctx, "pT", [P, 5, P])
                o2T = sb(ctx, "o2T", [P, P])
                fo = sb(ctx, "fo", [P, TT, HD])
                fsq = sb(ctx, "fsq", [P, TT, HD])
                fss = sb(ctx, "fss", [P, TT])
                frs = sb(ctx, "frs", [P, TT])
                block = ctx.enter_context(nc.Block())
                qT, kT = qkT[:, 0, :], qkT[:, 1, :]

                def fox_pe(pe, h):
                    def W(name):
                        pe.wait_ge(sem(name), h + 1)
                    pe.wait_ge(sem("f_buf"), TT * (h + 1))
                    for t in range(TT):
                        last = nc.tensor.transpose(b3[:, t * P:(t + 1) * P], fbuf[:, t, 0:HD], ident)
                    last.then_inc(sem("f_qT_ps"), 1)
                    yield
                    for t in range(TT):
                        last = nc.tensor.transpose(b4[:, t * P:(t + 1) * P], fbuf[:, t, HD:2 * HD], ident)
                    last.then_inc(sem("f_kT_ps"), 1)
                    yield
                    pe.wait_ge(sem("kc_in"), 16 * (h + 1))
                    for b in range(4):
                        last = nc.tensor.transpose(b5[:, b * P:(b + 1) * P], kc[:, b, :], ident)
                    last.then_inc(sem("f_kcT_ps0"), 1)
                    yield
                    for b in range(4):
                        last = nc.tensor.transpose(b6[:, b * P:(b + 1) * P], kc[:, 4 + b, :], ident)
                    last.then_inc(sem("f_kcT_ps1"), 1)
                    yield
                    W("f_qT"), W("f_kT"), W("f_nch")
                    one8 = ones[0:HEADS, :]
                    nc.tensor.matmul(b3[:, 0:2 * P], qT[:, P:2 * P], kT[:, 0:2 * P], start=True, stop=False)
                    nc.tensor.matmul(b3[:, 0:2 * P], one8, nch[:, 0:2 * P], start=False, stop=True)
                    nc.tensor.matmul(b3[:, 2 * P:3 * P], qT[:, 0:P], kT[:, 0:P], start=True, stop=False)
                    nc.tensor.matmul(b3[:, 2 * P:3 * P], one8, nch[:, 0:P], start=False, stop=True)\
                        .then_inc(sem("f_sp_ps"), 1)
                    yield
                    nc.tensor.matmul(b4[:, P:2 * P], qT[:, 2 * P:], kT[:, 2 * P:], start=True, stop=False)
                    nc.tensor.matmul(b4[:, P:2 * P], one8, nch[:, 2 * P:], start=False, stop=True)
                    W("f_kcT0"), W("f_kcT1")
                    for b in range(NB):
                        c = slice(b * NQ, (b + 1) * NQ)
                        last = nc.tensor.matmul(b7[:, c], kcT[:, b * HD:(b + 1) * HD],
                                                qT[:, 2 * P + b * NQ:2 * P + (b + 1) * NQ], start=True, stop=True)
                    last.then_inc(sem("f_scT_ps"), 1)
                    yield
                    W("f_scT")
                    nc.tensor.transpose(b4[:, 0:P], scT[:], ident).then_inc(sem("f_ss_ps"), 1)
                    yield
                    yield
                    yield
                    W("f_p")
                    for j, (t, c) in enumerate(((0, 0), (1, 0), (1, P), (2, P))):
                        last = nc.tensor.transpose(b6[:, j * P:(j + 1) * P], sc[:, t, c:c + P], ident)
                    last.then_inc(sem("f_pT_ps0"), 1)
                    nc.tensor.transpose(b7[:, 0:P], sc[:, 2, 0:P], ident).then_inc(sem("f_pT_ps1"), 1)
                    yield
                    W("f_pT0"), W("f_pT1")
                    v = fbuf[:, :, 2 * HD:]
                    nc.tensor.matmul(b7[:, 0:P], v[:, 2, :], pT[:, 3, :], start=True, stop=False)
                    pe.wait_ge(sem("vc_in"), 16 * (h + 1))
                    for b in range(NB):
                        c = slice(b * NQ, (b + 1) * NQ)
                        last = nc.tensor.matmul(b7[:, c], vc[:, b, :], pT[:, 4, c], start=False, stop=(b == NB - 1))
                    last.then_inc(sem("f_o2_ps"), 1)
                    yield
                    nc.tensor.matmul(b5[:, 0:P], pT[:, 0, :], v[:, 0, :], start=True, stop=True)
                    nc.tensor.matmul(b5[:, P:2 * P], pT[:, 1, :], v[:, 0, :], start=True, stop=False)
                    nc.tensor.matmul(b5[:, P:2 * P], pT[:, 2, :], v[:, 1, :], start=False, stop=True)
                    W("f_o2T")
                    nc.tensor.transpose(b5[:, 2 * P:3 * P], o2T[:], ident).then_inc(sem("f_o_ps"), 1)
                    yield
                    yield
                    yield
                    W("f_o")
                    for t in range(TT):
                        last = nc.tensor.transpose(b3[:, t * P:(t + 1) * P], fo[:, t, :], ident)
                    last.then_inc(sem("f_oT_ps"), 1)
                    yield
                    W("f_mix")

                def fox_act(act, h):
                    def W(name):
                        act.wait_ge(sem(name), h + 1)
                    yield 0
                    W("f_qT_ps")
                    nc.scalar.activation(qT, b3[:, 0:TOK], ACT.Copy, scale=SCALE).then_inc(sem("f_qT"), 1)
                    W("f_kcT_ps0")
                    nc.scalar.activation(kcT[:, 0:512], b5[:, :], ACT.Copy).then_inc(sem("f_kcT0"), 1)
                    yield 1
                    W("f_kcT_ps1")
                    nc.scalar.activation(kcT[:, 512:], b6[:, :], ACT.Copy).then_inc(sem("f_kcT1"), 1)
                    yield 2
                    W("f_max")
                    for t, w in ((0, P), (1, 2 * P), (2, 2 * P)):
                        last = nc.scalar.activation(sc[:, t, 0:w], sc[:, t, 0:w], ACT.Exp, bias=nmax[:, t:t + 1],
                                                    accum_out=den[:, t:t + 1])
                    last.then_inc(sem("f_p"), 1)
                    yield 3
                    W("f_pT_ps0")
                    nc.scalar.activation(pT[:, 0:4, :], tiles(b6[:, :], 4), ACT.Copy).then_inc(sem("f_pT0"), 1)
                    yield 4
                    W("f_ms")
                    rsqrt_act(act, frs[:], fss[:], "f_ln", h + 1, "f_rs")
                    yield 5
                    W("f_oT_ps")
                    nc.scalar.activation(mixT_hi[:, bass.ds(h, 1), :], b3[:, 0:TOK].unsqueeze(1), ACT.Copy, scale=nwf[:])\
                        .then_inc(sem("f_mix_hi"), 1)

                def fox_dve(dve, h):
                    def W(name):
                        dve.wait_ge(sem(name), h + 1)

                    own = [0]

                    def after(ins):
                        own[0] += 1
                        ins.then_inc(sem("f_own"), 1)
                        dve.wait_ge(sem("f_own"), F_OWN * h + own[0])
                    yield 0
                    nc.vector.tensor_scalar(nch[:], ncT[:], cn[0:HEADS, bass.ds(C_ID + h, 1)], None, ALU.mult)\
                        .then_inc(sem("f_nch"), 1)
                    W("f_kT_ps")
                    nc.vector.tensor_copy(kT, b4[:, 0:TOK]).then_inc(sem("f_kT"), 1)
                    yield 1
                    W("f_sp_ps")
                    nc.vector.scalar_tensor_tensor(
                        out=sc[:, 1, :], in0=b3[:, 0:2 * P], scalar=cfox[:, 1, bass.ds(h, 1)],
                        in1=cn[:, C_MP:C_MP + 2 * P], op0=ALU.add, op1=ALU.add)
                    nc.vector.scalar_tensor_tensor(
                        out=sc[:, 0, 0:P], in0=b3[:, 2 * P:3 * P], scalar=cfox[:, 0, bass.ds(h, 1)],
                        in1=cn[:, C_MP + P:C_MP + 2 * P], op0=ALU.add, op1=ALU.add)
                    W("f_scT_ps")
                    nc.vector.tensor_tensor(
                        scT[:].rearrange("p (b q) -> p b q", b=NB), b7[:, 0:P].rearrange("p (b q) -> p b q", b=NB),
                        ccache[:, :, bass.ds(h, 1)].broadcast_to([P, NB, NQ]), ALU.subtract)\
                        .then_inc(sem("f_scT"), 1)
                    yield 2
                    W("f_ss_ps")
                    after(nc.vector.scalar_tensor_tensor(
                        out=sc[:, 2, :], in0=b4[:, 0:2 * P], scalar=cfox[:, 2, bass.ds(h, 1)],
                        in1=cn[:, C_MS:C_MS + 2 * P], op0=ALU.add, op1=ALU.add))
                    for t, w in ((0, P), (1, 2 * P), (2, 2 * P)):
                        last = nc.vector.tensor_reduce(nmax[:, t:t + 1], sc[:, t, 0:w], AX, ALU.max, negate=True)
                    last.then_inc(sem("f_max"), 1)
                    yield 3
                    W("f_p")
                    nc.vector.reciprocal(rden[:], den[:]).then_inc(sem("f_rden"), 1)
                    W("f_pT_ps1")
                    nc.vector.tensor_copy(pT[:, 4, :], b7[:, 0:P]).then_inc(sem("f_pT1"), 1)
                    W("f_o2_ps")
                    nc.vector.tensor_copy(o2T[:], b7[:, 0:P]).then_inc(sem("f_o2T"), 1)
                    yield 4
                    W("f_o_ps"), W("f_rden")
                    for t in range(TT):
                        last = nc.vector.tensor_scalar(fo[:, t, :], b5[:, t * P:(t + 1) * P], rden[:, t:t + 1], None,
                                                       ALU.mult)
                    after(last)
                    for t in range(TT):
                        last = nc.vector.scalar_tensor_tensor(
                            out=fsq[:, t, :], in0=fo[:, t, :], scalar=1.0, in1=fo[:, t, :], op0=ALU.mult,
                            op1=ALU.mult, accum_out=fss[:, t:t + 1])
                    after(last)
                    nc.vector.tensor_scalar(fss[:], fss[:], 1.0 / HD, 1e-6, ALU.mult, ALU.add)\
                        .then_inc(sem("f_ms"), 1)
                    W("f_rs")
                    polish(frs[:], fss[:], pol[:], after)
                    for t in range(TT):
                        last = nc.vector.tensor_scalar(fo[:, t, :], fo[:, t, :], frs[:, t:t + 1], None, ALU.mult)
                    last.then_inc(sem("f_o"), 1)
                    yield 5
                    W("f_mix_hi")
                    nc.vector.scalar_tensor_tensor(
                        out=mixT_lo[:, bass.ds(h, 1), :], in0=b3[:, 0:TOK].unsqueeze(1), scalar=nwf[:],
                        in1=mixT_hi[:, bass.ds(h, 1), :], op0=ALU.mult, op1=ALU.subtract).then_inc(sem("f_mix"), 1)
                    assert own[0] == F_OWN

                def fox_evac(act, h, t):
                    wait_acc(act, "acc", h, t, G_FOX + NP_IN * (h + 1))
                    nc.scalar.activation(fbuf[:, t, :], bank[t][:, 0:3 * HD], ACT.Copy)\
                        .then_inc(sem("f_buf"), 1)
                    act.wait_ge(sem("f_buf"), TT * h + t + 1)
                    act.sem_inc(sem("acc_free"), 1)

                def gdn_evac(act, h, t):
                    wait_acc(act, "acc", HEADS + h, t, G_GDN + NP_IN * (h + 1))
                    nc.scalar.activation(gbuf[:, t, :], bank[t][:, :], ACT.Copy).then_inc(sem("g_buf"), 1)
                    act.wait_ge(sem("g_buf"), TT * h + t + 1)
                    act.sem_inc(sem("acc_free"), 1)

                @block.sync
                def _(sp):
                    for n in range(RAW + RING, NP_IN):
                        loads(sp, n, n % RAW, fox_parts(0, n, n % RAW))
                    with sp.Fori(0, HEADS - 1) as i:
                        for n in range(NP_IN):
                            loads(sp, NP_IN + n + NP_IN * i, n % RAW, fox_parts(i + 1, n, n % RAW))
                    for n in range(NP_IN + RAW + RING):
                        h, m = divmod(n, NP_IN)
                        loads(sp, G_GDN + n, n % RAW, gdn_parts(h, m, n % RAW))

                @block.gpsimd
                def _(pool):
                    def load_cache(dst, src, h, name):
                        pool.dma_start(dst[:], src[0, :, :, bass.ds(h, 1), :].rearrange("b t o d -> t b (o d)"))\
                            .then_inc(sem(name), 16)

                    def store(h, last):
                        pool_wait(pool, sem("f_buf"), TT * (h + 1))
                        for part, prompt, sample in ((1, o_kp, o_ks), (2, o_vp, o_vs)):
                            c = slice(part * HD, (part + 1) * HD)
                            pool.dma_start(prompt[0, 0, :, bass.ds(h, 1), :].rearrange("(t p) o d -> p t (o d)", p=P),
                                           fbuf[:, 0:2, c]).then_inc(sem("f_stored"), 16)
                            pool.dma_start(sample[0, :, :, bass.ds(h, 1), :].rearrange("b s o d -> (b s) (o d)"),
                                           fbuf[:, 2, c]).then_inc(sem("f_stored"), 16)
                        if not last:
                            pool_wait(pool, sem("f_kcT_ps1"), h + 1)
                            load_cache(kc, cache_k, h + 1, "kc_in")
                            pool_wait(pool, sem("f_o2_ps"), h + 1)
                            load_cache(vc, cache_v, h + 1, "vc_in")
                    load_cache(kc, cache_k, 0, "kc_in")
                    load_cache(vc, cache_v, 0, "vc_in")
                    with pool.Fori(0, HEADS - 1) as i:
                        store(i, False)
                    store(HEADS - 1, True)
                    pool_wait(pool, sem("f_stored"), 64 * HEADS)

                def act_block(act, g0, i, per, mixer, evac):
                    for n in range(NP_IN):
                        if mixer is not None:
                            mixer.upto(n if n < NP_IN - 1 else None)
                        if n == NP_IN - 1:
                            for t in range(TT):
                                evac(t)
                        split_act(act, g0 + RING, n, i, per)

                def dve_block(dve, g0, i, per, mixer):
                    for n in range(NP_IN):
                        if mixer is not None:
                            mixer.upto(n if n < NP_IN - 1 else None)
                        split_dve(dve, g0 + RING, n, i, per)

                @block.scalar
                def _(act):
                    act_block(act, G_FOX, 0, 0, None, lambda t: fox_evac(act, 0, t))
                    with act.Fori(0, HEADS - 1) as i:
                        act_block(act, G_FOX + NP_IN, i, NP_IN, Course(fox_act(act, i)), lambda t: (
                            act.wait_ge(sem("f_stored"), 64 * (i + 1)), fox_evac(act, i + 1, t)))
                    act_block(act, G_GDN, 0, 0, Course(fox_act(act, HEADS - 1)), lambda t: gdn_evac(act, 0, t))

                @block.vector
                def _(dve):
                    def stored(h):
                        dve.wait_ge(sem("f_stored"), 64 * (h + 1))
                    dve_block(dve, G_FOX, 0, 0, None)
                    with dve.Fori(0, HEADS - 1) as i:
                        dve_block(dve, G_FOX + NP_IN, i, NP_IN, Course(fox_dve(dve, i)))
                    dve_block(dve, G_GDN, 0, 0, Course(fox_dve(dve, HEADS - 1)))

                @block.tensor
                def _(pe):
                    gemm(pe, G_FOX, NP_IN, aT_hi, aT_lo, 0, 3 * HD, ACC, "acc", 0, first=True)
                    with pe.Fori(0, HEADS - 1) as i:
                        gemm(pe, G_FOX + NP_IN, NP_IN, aT_hi, aT_lo, 0, 3 * HD, ACC, "acc", 1, i, NP_IN, 1,
                             fox_pe(pe, i))
                    gemm(pe, G_GDN, NP_IN, aT_hi, aT_lo, 0, CW, ACC, "acc", HEADS, between=fox_pe(pe, HEADS - 1))

            with ExitStack() as ctx:
                early = sb(ctx, "early", [P, 3 * SEG * (NQ + 3)])
                ext = early[:].rearrange("p (a s q) -> p a s q", a=3, s=SEG)
                A, B, T = (early[:, n * TOK:(n + 1) * TOK].rearrange("p (t c) -> p t c", t=TT) for n in range(3))
                cv = sb(ctx, "cv", [P, 3, TOK])
                R, vn, oq = (cv[:, n, :].rearrange("p (t c) -> p t c", t=TT) for n in range(3))
                nq = sb(ctx, "nq", [P, 3, TT, HD])
                ke = sb(ctx, "ke", [P, TT, HD])
                gT2 = sb(ctx, "g_kqT", [P, 2, TOK])
                dec = sb(ctx, "dec", [P, TT, P])
                go = dec
                U = sb(ctx, "U", [P, TT, P])
                qkd = sb(ctx, "qkd", [P, TT, P])
                Z = qkd
                qkdT = sb(ctx, "qkdT", [P, TT, P])
                S = sb(ctx, "S", [P, NB, HD])
                vm = sb(ctx, "vm", [P, NB, HD])
                flat = vm[:].rearrange("p b c -> p (b c)")
                ngh, ksT = flat[0:HEADS, 0:TOK], flat[:, 512:768].rearrange("p (a c) -> p a c", a=2)
                S1 = sb(ctx, "S1", [P, HD])
                gss = sb(ctx, "gss", [P, TT])
                nss = sb(ctx, "nss", [P, 2, TT])
                nrs = sb(ctx, "nrs", [P, 2, TT])
                npol = sb(ctx, "npol", [P, 2, TT])
                grs = sb(ctx, "grs", [P, TT])
                zg = gbuf[:, :, 0:HD]
                block = ctx.enter_context(nc.Block())
                kTn, qTn = gT2[:, 0, :], gT2[:, 1, :]
                cvb = (b3, b4, b5)
                lv = [cn[:, C_LV + n * P:C_LV + (n + 1) * P] for n in range(LEVELS)]

                def n_tiles(level):
                    return TT if (1 << level) < NQ else 2

                def tl(x, t, c=P):
                    return x[:, t * c:(t + 1) * c]

                def gdn_pe(pe, h):
                    def W(name):
                        pe.wait_ge(sem(name), h + 1)

                    def L(name, n, per_head):
                        pe.wait_ge(sem(name), per_head * h + n)
                    pe.wait_ge(sem("g_buf"), TT * (h + 1))
                    for a in range(3):
                        for t in range(TT):
                            last = nc.tensor.transpose(tl(cvb[a], t), gbuf[:, t, a * HD:(a + 1) * HD], ident)
                        last.then_inc(sem("g_raw_ps"), 1)
                    yield
                    yield
                    yield
                    yield
                    for a, bk in enumerate((b6, b7, b3)):
                        L("g_cv", a + 1, 3)
                        for t in range(TT):
                            last = nc.tensor.transpose(tl(bk, t), tl(cv[:, a, :], t), ident)
                        last.then_inc(sem("g_tok_ps"), 1)
                        yield
                    yield
                    W("g_nq")
                    for t in range(TT):
                        last = nc.tensor.transpose(tl(b4, t), nq[:, 0, t, :], ident)
                    last.then_inc(sem("g_qT_ps"), 1)
                    W("g_nk")
                    for t in range(TT):
                        last = nc.tensor.transpose(tl(b5, t), nq[:, 1, t, :], ident)
                    last.then_inc(sem("g_kT_ps"), 1)
                    yield
                    W("g_qT"), W("g_kT"), W("g_ngh"), W("g_nv")
                    nc.tensor.matmul(b3[:, 0:TOK], ones[0:HEADS, :], ngh, start=True, stop=True)\
                        .then_inc(sem("g_dec_ps"), 1)
                    for t in range(TT):
                        last = nc.tensor.matmul(tl(b6, t), tl(kTn, t), tl(kTn, t), start=True, stop=True)
                    last.then_inc(sem("g_kk_ps"), 1)
                    for t in range(TT):
                        last = nc.tensor.matmul(tl(b7, t), tl(qTn, t), tl(kTn, t), start=True, stop=True)
                    last.then_inc(sem("g_qk_ps"), 1)
                    yield
                    pe.wait_ge(sem("g_S_in"), 16 * (h + 1))
                    for b in range(NB):
                        last = nc.tensor.matmul(b4[:, 0:2 * P].rearrange("p (a c) -> p a c", a=2)[:, :, b * NQ:(b + 1) * NQ],
                                                S[:, b, :], gT2[:, :, 2 * P + b * NQ:2 * P + (b + 1) * NQ],
                                                start=True, stop=True)
                    last.then_inc(sem("g_ksT_ps"), 1)
                    yield
                    W("g_T1")
                    for t in range(TT):
                        last = nc.tensor.transpose(tl(b5, t), T[:, t, :], ident)
                    last.then_inc(sem("g_U1_ps"), 1)
                    W("g_qkd")
                    for t in range(TT):
                        last = nc.tensor.transpose(tl(b3, t), qkd[:, t, :], ident)
                    last.then_inc(sem("g_qkdT_ps"), 1)
                    W("g_ksT")
                    for a in range(2):
                        last = nc.tensor.transpose(b7[:, a * P:(a + 1) * P], ksT[:, a, :], ident)
                    last.then_inc(sem("g_ks_ps"), 1)
                    yield
                    for n in range(1, LEVELS):
                        L("g_U", n, LEVELS), L("g_B", n, LEVELS - 1)
                        for t in range(n_tiles(n)):
                            last = nc.tensor.matmul(tl(b6, t), B[:, t, :], U[:, t, :], start=True, stop=True)
                        last.then_inc(sem("g_Z_ps"), 1)
                        if n > 1:
                            for t in range(n_tiles(n)):
                                last = nc.tensor.transpose(tl(b4, t), U[:, t, :], ident)
                            last.then_inc(sem("g_T_ps"), 1)
                        yield
                        L("g_Z", n, LEVELS - 1)
                        if n > 1:
                            L("g_Tl", n - 1, LEVELS - 2)
                        for t in range(n_tiles(n)):
                            last = nc.tensor.matmul(tl(b5, t), T[:, t, :], Z[:, t, :], start=True, stop=True)
                        last.then_inc(sem("g_UZ_ps"), 1)
                        yield
                    L("g_U", LEVELS, LEVELS), W("g_R2"), W("g_qkdT")
                    nc.tensor.matmul(tl(b6, 0), U[:, 0, :], nq[:, 2, 0, :], start=True, stop=True)
                    nc.tensor.matmul(tl(b6, 2), U[:, 2, :], R[:, 2, :], start=True, stop=True)\
                        .then_inc(sem("g_v02_ps"), 1)
                    yield
                    W("g_v02"), W("g_ke")
                    nc.tensor.matmul(tl(b4, 0), ke[:, 0, :], vn[:, 0, :], start=True, stop=True)\
                        .then_inc(sem("g_S1_ps"), 1)
                    nc.tensor.matmul(tl(b7, 0), qkdT[:, 0, :], vn[:, 0, :], start=True, stop=True)
                    nc.tensor.matmul(tl(b7, 2), qkdT[:, 2, :], vn[:, 2, :], start=True, stop=True)
                    yield
                    W("g_S1")
                    nc.tensor.matmul(b5[:, 0:P], tl(kTn, 1), S1[:], start=True, stop=True)
                    nc.tensor.matmul(b5[:, P:2 * P], tl(qTn, 1), S1[:], start=True, stop=True)\
                        .then_inc(sem("g_ks1_ps"), 1)
                    yield
                    W("g_R1")
                    nc.tensor.matmul(tl(b6, 0), U[:, 1, :], R[:, 1, :], start=True, stop=True)\
                        .then_inc(sem("g_v1_ps"), 1)
                    yield
                    W("g_vm")
                    nc.tensor.matmul(b3[:, :], ke[:, 2, :], vm[:, 0:4, :].rearrange("p b c -> p (b c)"), start=True,
                                     stop=True)
                    W("g_v1")
                    nc.tensor.matmul(tl(b7, 1), qkdT[:, 1, :], vn[:, 1, :], start=True, stop=True)\
                        .then_inc(sem("g_o_ps"), 1)
                    nc.tensor.matmul(b4[:, 0:P], ke[:, 1, :], vn[:, 1, :], start=True, stop=True)\
                        .then_inc(sem("g_S2_ps"), 1)
                    W("g_R1")
                    nc.tensor.matmul(b5[:, :], ke[:, 2, :], vm[:, 4:8, :].rearrange("p b c -> p (b c)"), start=True,
                                     stop=True).then_inc(sem("g_Ss_ps"), 1)
                    yield
                    yield
                    W("g_o")
                    for t in range(TT):
                        last = nc.tensor.transpose(tl(b6, t), go[:, t, :], ident)
                    last.then_inc(sem("g_oT_ps"), 1)
                    yield
                    W("g_mix"), W("g_state")

                def gdn_act(act, h):
                    def W(name):
                        act.wait_ge(sem(name), h + 1)

                    def L(name, n, per_head):
                        act.wait_ge(sem(name), per_head * h + n)
                    yield 0
                    for a in range(3):
                        L("g_raw_ps", a + 1, 3)
                        nc.scalar.activation(ext[:, a, :, 3:], cvb[a][:, 0:TOK].rearrange("p (s q) -> p s q", q=NQ),
                                             ACT.Copy).then_inc(sem("g_ext"), 1)
                    yield 0
                    for a in range(3):
                        yield (a + 1) // 2
                        L("g_sum", a + 1, 3)
                        nc.scalar.activation(cvb[a][:, 0:TOK], cv[:, a, :], ACT.Tanh, scale=0.5)\
                            .then_inc(sem("g_th"), 1)
                    yield 1
                    act.wait_ge(sem("g_rows_out"), 16 * (NB + 1) * (h + 1))
                    nc.scalar.activation(zg, gbuf[:, :, 3 * HD:], ACT.Tanh, scale=0.5).then_inc(sem("g_thz"), 1)
                    yield 2
                    for a, bk in enumerate((b6, b7)):
                        L("g_tok_ps", a + 1, 3)
                        for t in range(TT):
                            last = nc.scalar.activation((qkd, qkdT)[a][:, t, :], tl(bk, t), ACT.Square, accum_out=nss[:, a, t:t + 1])
                        last.then_inc(sem("g_ss"), 1)
                    W("g_ms")
                    rsqrt_act(act, nrs[:], nss[:], "g_ln", 2 * h + 1, "g_rs")
                    W("g_pol")
                    for t in range(TT):
                        last = nc.scalar.activation(nq[:, 0, t, :], tl(b6, t), ACT.Copy, scale=nrs[:, 0, t:t + 1])
                    last.then_inc(sem("g_nq"), 1)
                    yield 3
                    W("g_qT_ps")
                    nc.scalar.activation(qTn, b4[:, 0:TOK], ACT.Copy).then_inc(sem("g_qT"), 1)
                    W("g_decin")
                    nc.scalar.activation(dec[:], dec[:], ACT.Exp).then_inc(sem("g_dec"), 1)
                    W("g_ksT_ps")
                    nc.scalar.activation(ksT, b4[:, 0:2 * P].rearrange("p (a c) -> p a c", a=2), ACT.Copy)\
                        .then_inc(sem("g_ksT"), 1)
                    yield 4
                    W("g_U1_ps")
                    nc.scalar.activation(U[:], tiles(b5[:, 0:TOK]), ACT.Copy).then_inc(sem("g_U"), 1)
                    W("g_qkdT_ps")
                    nc.scalar.activation(qkdT[:], tiles(b3[:, 0:TOK]), ACT.Copy).then_inc(sem("g_qkdT"), 1)
                    for n in range(2, LEVELS):
                        yield (13 + 2 * (n - 1)) // 3
                        m = n_tiles(n)
                        L("g_T_ps", n - 1, LEVELS - 2)
                        nc.scalar.activation(T[:, 0:m, :], tiles(b4[:, 0:m * P], m), ACT.Copy)\
                            .then_inc(sem("g_Tl"), 1)
                    yield 8
                    W("g_S1_ps")
                    nc.scalar.activation(S1[:], b4[:, 0:P], ACT.Copy).then_inc(sem("g_S1"), 1)
                    yield 10
                    W("g_oms")
                    rsqrt_act(act, grs[:], gss[:], "g_ln", 2 * h + 2, "g_ors")
                    W("g_oT_ps")
                    nc.scalar.activation(mixT_hi[:, bass.ds(h + HEADS, 1), :], b6[:, 0:TOK].unsqueeze(1), ACT.Copy,
                                         scale=nwg2[:]).then_inc(sem("g_mix_hi"), 1)

                def gdn_dve(dve, h):
                    V = nc.vector

                    def W(name):
                        dve.wait_ge(sem(name), h + 1)

                    def L(name, n, per_head):
                        dve.wait_ge(sem(name), per_head * h + n)

                    own = [0]

                    def after(ins):
                        own[0] += 1
                        ins.then_inc(sem("g_own"), 1)
                        L("g_own", own[0], G_OWN)

                    def col(x, t):
                        return x[:, t, bass.ds(h, 1)]
                    yield 0
                    V.tensor_scalar(ngh, nGT[:], cn[0:HEADS, bass.ds(C_ID + h, 1)], None, ALU.mult)\
                        .then_inc(sem("g_ngh"), 1)
                    for a in range(3):
                        yield a // 2
                        L("g_ext", a + 1, 3), W("g_pre")
                        out = cv[:, a, :].rearrange("p (s q) -> p s q", q=NQ)
                        for r in range(TAP):
                            w = cw[:, bass.ds(r * 24 + a * 8 + h, 1)]
                            src = ext[:, a, :, r:r + NQ]
                            if r == 0:
                                ins = V.tensor_scalar(out, src, w, None, ALU.mult)
                            else:
                                ins = V.scalar_tensor_tensor(out=out, in0=src, scalar=w, in1=out, op0=ALU.mult,
                                                             op1=ALU.add)
                            if r < TAP - 1:
                                after(ins)
                            else:
                                ins.then_inc(sem("g_sum"), 1)
                        if a > 0:
                            silu(dve, h, a - 1)
                    yield 2
                    silu(dve, h, 2)
                    L("g_ss", 2, 2)
                    for a, f in ((0, 1.0 * HD), (1, 1.0)):
                        ins = V.tensor_scalar(nss[:, a, :], nss[:, a, :], f, 4e-6 * f, ALU.mult, ALU.add)
                    ins.then_inc(sem("g_ms"), 1)
                    W("g_rs")
                    polish(nrs[:], nss[:], npol[:], after)
                    dve.sem_inc(sem("g_pol"), 1)
                    for t in range(TT):
                        ins = V.tensor_scalar(nq[:, 1, t, :], tl(b7, t), nrs[:, 1, t:t + 1], None, ALU.mult)
                    ins.then_inc(sem("g_nk"), 1)
                    L("g_tok_ps", 3, 3)
                    for t in range(TT):
                        ins = V.tensor_scalar(nq[:, 2, t, :], tl(b3, t), col(bhalf, t), None, ALU.mult)
                    ins.then_inc(sem("g_nv"), 1)
                    yield 3
                    W("g_kT_ps")
                    V.tensor_copy(kTn, b5[:, 0:TOK]).then_inc(sem("g_kT"), 1)
                    W("g_dec_ps")
                    for t in range(TT):
                        m = C_MP if t < 2 else C_MS
                        ins = V.scalar_tensor_tensor(out=dec[:, t, :], in0=tl(b3, t), scalar=col(Gc, t),
                                                     in1=cn[:, m + P:m + 2 * P], op0=ALU.add, op1=ALU.add)
                    ins.then_inc(sem("g_decin"), 1)
                    W("g_dec"), W("g_kk_ps")
                    for t in range(TT):
                        ins = V.scalar_tensor_tensor(out=A[:, t, :], in0=tl(b6, t), scalar=col(beta, t),
                                                     in1=dec[:, t, :], op0=ALU.mult, op1=ALU.mult)
                    after(ins)
                    after(V.tensor_tensor(B, A, lv[0].unsqueeze(1).broadcast_to([P, TT, P]), ALU.mult))
                    V.tensor_tensor(T, ident.unsqueeze(1).broadcast_to([P, TT, P]), B, ALU.subtract)\
                        .then_inc(sem("g_T1"), 1)
                    W("g_qk_ps")
                    V.tensor_tensor(qkd[:], tiles(b7[:, 0:TOK]), dec[:], ALU.mult).then_inc(sem("g_qkd"), 1)
                    W("g_T1")
                    V.tensor_tensor(B, A, lv[1].unsqueeze(1).broadcast_to([P, TT, P]), ALU.mult)\
                        .then_inc(sem("g_B"), 1)
                    yield 4
                    W("g_ks_ps")
                    V.scalar_tensor_tensor(out=R[:, 2, :], in0=b7[:, 0:P], scalar=col(nbe, 2), in1=nq[:, 2, 2, :],
                                           op0=ALU.mult, op1=ALU.add).then_inc(sem("g_R2"), 1)
                    V.tensor_scalar(oq[:, 2, :], b7[:, P:2 * P], col(eG, 2), None, ALU.mult).then_inc(sem("g_oq2"), 1)
                    for n in range(1, LEVELS):
                        yield (13 + 2 * (n - 1)) // 3
                        m = n_tiles(n)
                        L("g_Z_ps", n, LEVELS - 1)
                        V.tensor_copy(Z[:, 0:m, :], tiles(b6[:, 0:m * P], m)).then_inc(sem("g_Z"), 1)
                        if n + 1 < LEVELS:
                            V.tensor_tensor(B, A, lv[n + 1].unsqueeze(1).broadcast_to([P, TT, P]), ALU.mult)\
                                .then_inc(sem("g_B"), 1)
                        yield (14 + 2 * (n - 1)) // 3
                        L("g_UZ_ps", n, LEVELS - 1), L("g_U", n, LEVELS)
                        V.tensor_tensor(U[:, 0:m, :], U[:, 0:m, :], tiles(b5[:, 0:m * P], m), ALU.subtract)\
                            .then_inc(sem("g_U"), 1)
                    yield 8
                    W("g_v02_ps")
                    V.tensor_copy(vn[:, 0, :], tl(b6, 0))
                    V.tensor_copy(vn[:, 2, :], tl(b6, 2)).then_inc(sem("g_v02"), 1)
                    yield 9
                    W("g_ks1_ps")
                    V.scalar_tensor_tensor(out=R[:, 1, :], in0=b5[:, 0:P], scalar=col(nbe, 1), in1=nq[:, 2, 1, :],
                                           op0=ALU.mult, op1=ALU.add)
                    V.tensor_scalar(oq[:, 1, :], b5[:, P:2 * P], col(eG, 1), None, ALU.mult).then_inc(sem("g_R1"), 1)
                    W("g_v1_ps")
                    V.tensor_copy(vn[:, 1, :], tl(b6, 0)).then_inc(sem("g_v1"), 1)
                    yield 10
                    W("g_o_ps"), W("g_oq2")
                    V.tensor_copy(go[:, 0, :], tl(b7, 0))
                    after(V.tensor_tensor(go[:, 1:3, :], oq[:, 1:3, :], tiles(b7[:, P:3 * P], 2), ALU.add))
                    for t in range(TT):
                        ins = V.scalar_tensor_tensor(out=R[:, t, :], in0=go[:, t, :], scalar=1.0, in1=go[:, t, :],
                                                     op0=ALU.mult, op1=ALU.mult, accum_out=gss[:, t:t + 1])
                    after(ins)
                    V.tensor_scalar(gss[:], gss[:], 1.0 / HD, 1e-6, ALU.mult, ALU.add).then_inc(sem("g_oms"), 1)
                    W("g_thz")
                    after(V.scalar_tensor_tensor(out=zg, in0=zg, scalar=1.0, in1=gbuf[:, :, 3 * HD:],
                                                 op0=ALU.add, op1=ALU.mult))
                    W("g_ors")
                    polish(grs[:], gss[:], pol[:], after)
                    for t in range(TT):
                        ins = V.scalar_tensor_tensor(out=go[:, t, :], in0=go[:, t, :], scalar=grs[:, t:t + 1],
                                                     in1=zg[:, t, :], op0=ALU.mult, op1=ALU.mult)
                    ins.then_inc(sem("g_o"), 1)
                    W("g_S2_ps"), W("g_S1")
                    V.scalar_tensor_tensor(out=S1[:], in0=S1[:], scalar=eL[:, 1, bass.ds(h, 1)], in1=b4[:, 0:P],
                                           op0=ALU.mult, op1=ALU.add)
                    W("g_Ss_ps"), W("g_Sdec")
                    V.tensor_tensor(S[:, 0:4, :], S[:, 0:4, :], tiles(b3[:, :], 4), ALU.add)
                    V.tensor_tensor(S[:, 4:8, :], S[:, 4:8, :], tiles(b5[:, :], 4), ALU.add)\
                        .then_inc(sem("g_state"), 1)
                    W("g_mix_hi")
                    V.scalar_tensor_tensor(out=mixT_lo[:, bass.ds(h + HEADS, 1), :], in0=b6[:, 0:TOK].unsqueeze(1),
                                           scalar=nwg2[:], in1=mixT_hi[:, bass.ds(h + HEADS, 1), :], op0=ALU.mult,
                                           op1=ALU.subtract).then_inc(sem("g_mix"), 1)
                    assert own[0] == G_OWN

                def silu(dve, h, a):
                    dve.wait_ge(sem("g_th"), 3 * h + a + 1)
                    nc.vector.scalar_tensor_tensor(out=cv[:, a, :], in0=cvb[a][:, 0:TOK], scalar=1.0,
                                                   in1=cv[:, a, :], op0=ALU.add, op1=ALU.mult)\
                        .then_inc(sem("g_cv"), 1)

                def gdn_pool(pool, h, last):
                    G = nc.gpsimd

                    def W(name):
                        pool_wait(pool, sem(name), h + 1)
                    pool_wait(pool, sem("g_buf"), TT * (h + 1))
                    pool.dma_start(o_cp[0, 0].rearrange("r (a g c) -> r a g c", a=3, c=HD)[:, :, bass.ds(h, 1), :]
                                   .rearrange("r a o c -> r a (o c)"),
                                   gbuf[P - 3:P, 1, 0:3 * HD].rearrange("p (a c) -> p a c", a=3))\
                        .then_inc(sem("g_rows_out"), 16)
                    for b in range(NB):
                        pool.dma_start(
                            o_cs[0, b].rearrange("r (a g c) -> r a g c", a=3, c=HD)[:, :, bass.ds(h, 1), :]
                            .rearrange("r a o c -> r a (o c)"),
                            gbuf[(b + 1) * NQ - 3:(b + 1) * NQ, 2, 0:3 * HD].rearrange("p (a c) -> p a c", a=3))\
                            .then_inc(sem("g_rows_out"), 16)
                    pool_wait(pool, sem("g_ext"), 3 * (h + 1))
                    G.memset(ext[:, :, 0, 0:3], 0.0)
                    for a in range(3):
                        G.tensor_copy(ext[:, a, 1:2 * P // NQ, 0:3], ext[:, a, 0:2 * P // NQ - 1, NQ:NQ + 3])
                        ins = G.tensor_copy(ext[:, a, 2 * P // NQ:, 0:3],
                                            cprev[:, bass.ds(a * 8 + h, 1), :].rearrange("p o (b r) -> p (o b) r", r=3))
                    ins.then_inc(sem("g_pre"), 1)
                    W("g_nk")
                    G.tensor_tensor(ke[:], nq[:, 1], per_token(eR, h), ALU.mult).then_inc(sem("g_ke"), 1)
                    W("g_ksT_ps")
                    G.tensor_tensor(S[:], S[:], per_token(eL[:, 2:, :], h, NB), ALU.mult).then_inc(sem("g_Sdec"), 1)
                    W("g_v02")
                    G.tensor_tensor(vm[:], vn[:, 2, :].unsqueeze(1).broadcast_to([P, NB, HD]),
                                    cn[:, C_BM:C_BM + NB].unsqueeze(2).broadcast_to([P, NB, HD]), ALU.mult)\
                        .then_inc(sem("g_vm"), 1)
                    W("g_state")
                    pool.dma_start(o_sp[0, 0, bass.ds(h, 1)].rearrange("o k v -> (o k) v"), S1[:])\
                        .then_inc(sem("g_S_out"), 16)
                    pool.dma_start(o_ss[0, :, bass.ds(h, 1)].rearrange("b o k v -> k b (o v)"), S[:])\
                        .then_inc(sem("g_S_out"), 16)
                    pool_wait(pool, sem("g_S_out"), 32 * (h + 1))
                    pool_wait(pool, sem("g_rows_out"), 16 * (NB + 1) * (h + 1))
                    if not last:
                        load_state(pool, h + 1)
                    pool.sem_inc(sem("g_pool"), 1)

                def load_state(pool, h):
                    pool.dma_start(S[:], state_gdn[0, :, bass.ds(h, 1)].rearrange("b o k v -> k b (o v)"))\
                        .then_inc(sem("g_S_in"), 16)

                @block.sync
                def _(sp):
                    for n in range(NP_IN + RAW + RING, 2 * NP_IN):
                        loads(sp, G_GDN + n, n % RAW, gdn_parts(1, n - NP_IN, n % RAW))
                    with sp.Fori(0, HEADS - 2) as i:
                        for n in range(NP_IN):
                            loads(sp, G_GDN + 2 * NP_IN + n + NP_IN * i, n % RAW, gdn_parts(i + 2, n, n % RAW))
                    for n in range(NP_HALF):
                        loads(sp, G_OUT_FOX + n, n % RAW, plain_parts(w_out, n * KP * P, 0, n % RAW,
                                                                      dmas_of(G_OUT_FOX + n)))
                    with sp.Fori(1, NCB) as c:
                        for n in range(NP_HALF):
                            loads(sp, G_OUT_FOX + n + NP_HALF * c, n % RAW,
                                  plain_parts(w_out, n * KP * P, c * CW, n % RAW))
                    with sp.Fori(0, NCB) as c:
                        for n in range(NP_HALF):
                            loads(sp, G_OUT_GDN + n + NP_HALF * c, n % RAW,
                                  plain_parts(w_out, (NP_HALF + n) * KP * P, c * CW, n % RAW))
                    for n in range(RAW + RING):
                        loads(sp, G_UP0 + n, n % RAW, plain_parts(w_gate, n * KP * P, 0, n % RAW))

                @block.gpsimd
                def _(pool):
                    load_state(pool, 0)
                    with pool.Fori(0, HEADS - 1) as i:
                        gdn_pool(pool, i, False)
                    gdn_pool(pool, HEADS - 1, True)

                @block.scalar
                def _(act):
                    with act.Fori(0, HEADS - 1) as i:
                        act_block(act, G_GDN + NP_IN, i, NP_IN, Course(gdn_act(act, i)), lambda t: (
                            act.wait_ge(sem("g_pool"), i + 1), gdn_evac(act, i + 1, t)))
                    mixer = Course(gdn_act(act, HEADS - 1))
                    for n in range(NCB * NP_HALF):
                        mixer.upto(n)
                        split_act(act, G_OUT_FOX + RING, n)
                    with act.Fori(0, NCB) as c:
                        for n in range(NP_HALF):
                            split_act(act, G_OUT_GDN + RING, n, c, NP_HALF)

                def out_evac(dve, blk, c, t, scale):
                    wait_acc(dve, "acc", blk, t, G_OUT_FOX + NP_HALF * (blk - 2 * HEADS + 1))
                    xs = x_res[:, t, bass.ds(c * CW, CW)]
                    nc.vector.scalar_tensor_tensor(out=xs, in0=xs, scalar=scale, in1=bank[t][:, :], op0=ALU.mult,
                                                   op1=ALU.add).then_inc(sem("acc_free"), 1)

                @block.vector
                def _(dve):
                    with dve.Fori(0, HEADS - 1) as i:
                        dve_block(dve, G_GDN + NP_IN, i, NP_IN, Course(gdn_dve(dve, i)))
                    mixer = Course(gdn_dve(dve, HEADS - 1))
                    for n in range(NCB * NP_HALF):
                        c, m = divmod(n, NP_HALF)
                        mixer.upto(n)
                        if m == NP_HALF - 1:
                            for t in range(TT):
                                out_evac(dve, 2 * HEADS + c, c, t, ALPHA)
                        split_dve(dve, G_OUT_FOX + RING, n)
                    with dve.Fori(0, NCB) as c:
                        for n in range(NP_HALF):
                            if n == NP_HALF - 1:
                                for t in range(TT):
                                    out_evac(dve, 2 * HEADS + NCB + c, c, t, 1.0)
                            split_dve(dve, G_OUT_GDN + RING, n, c, NP_HALF)

                @block.tensor
                def _(pe):
                    with pe.Fori(0, HEADS - 1) as i:
                        gemm(pe, G_GDN + NP_IN, NP_IN, aT_hi, aT_lo, 0, CW, ACC, "acc", HEADS + 1, i, NP_IN, 1,
                             gdn_pe(pe, i))
                    mixer = gdn_pe(pe, HEADS - 1)
                    for c in range(NCB):
                        gemm(pe, G_OUT_FOX + NP_HALF * c, NP_HALF, mixT_hi, mixT_lo, 0, CW, ACC, "acc",
                             2 * HEADS + c, between=mixer, ends=c == NCB - 1)
                    with pe.Fori(0, NCB) as c:
                        gemm(pe, G_OUT_GDN, NP_HALF, mixT_hi, mixT_lo, HEADS, CW, ACC, "acc", 2 * HEADS + NCB, c,
                             NP_HALF, 1)

        BLK_MIX = 2 * HEADS + 2 * NCB
        with ExitStack() as ctx:
            gb = sb(ctx, "gb1", [P, 2, D])
            block = ctx.enter_context(nc.Block())

            @block.sync
            def _(sp):
                load_gb(sp, gb, ln_mix_g[0], ln_mix_b[0])

            @block.scalar
            def _(act):
                for r in range(ROUNDS):
                    if r % (ROUNDS // TT) == 0:
                        layer_norm_act(act, r // (ROUNDS // TT), 1)
                    x_evac_act(act, r, 1)

            @block.vector
            def _(dve):
                for t in range(TT):
                    layer_norm_dve(dve, t, gb, 1)
                    for r in range(t * 4, t * 4 + 4):
                        x_evac_dve(dve, r, 1)

            @block.tensor
            def _(pe):
                for r in range(ROUNDS):
                    x_transpose_pe(pe, r, 1)

        with ExitStack() as ctx:
            hT_hi = sb(ctx, "hT_hi", [P, KH, TOK], F32R)
            hT_lo = sb(ctx, "hT_lo", [P, KH, TOK], F32R)
            sg = sb(ctx, "sg", [P, TT, CW])
            hb = sb(ctx, "hb", [P, TT, CW])
            block = ctx.enter_context(nc.Block())

            def up_pe(pe, g0, j0, i):
                j = j0 + i
                per = 0 if isinstance(i, int) else 2 * NP_IN
                gemm(pe, g0, NP_IN, aT_hi, aT_lo, 0, CW, ACC, "acc", GATE_BLK(j0), i if per else 0, per, 1)
                gemm(pe, g0 + NP_IN, NP_IN, aT_hi, aT_lo, 0, CW, ACC2, "acc2", j0 + 1, i if per else 0, per, 1,
                     first=False)
                for t in range(TT):
                    pe.wait_ge(sem("h_ready"), TT * j + t + 1)
                    pe.wait_ge(sem("h_bank"), TT * j + t + 1)
                    for k in range(4):
                        last = nc.tensor.transpose(bank[6 + t % 2][:, k * P:(k + 1) * P],
                                                   hb[:, t, k * P:(k + 1) * P], ident)
                    last.then_inc(sem("h_ps"), 1)

            def GATE_BLK(j0):
                return BLK_MIX + j0 + (NCB if j0 else 0)

            def up_act(act, g0, j0, i):
                per = 0 if isinstance(i, int) else 2 * NP_IN
                ii = i if per else 0
                j = j0 + i
                for n in range(2 * NP_IN):
                    if n == NP_IN - 1:
                        for t in range(TT):
                            wait_acc(act, "acc", GATE_BLK(j0) + i, t, g0 + NP_IN + per * ii)
                            nc.scalar.activation(sg[:, t, :], bank[t][:, :], ACT.Tanh, scale=0.5)\
                                .then_inc(sem("sg_tanh"), 1)
                    split_act(act, g0 + RING, n, ii, per)
                for t in range(TT):
                    act.wait_ge(sem("h_ps"), TT * j + t + 1)
                    hk = hT_hi[:, bass.ds(4 * i, 4), t * P:(t + 1) * P]
                    nc.scalar.activation(hk, tiles4(bank[6 + t % 2]), ACT.Copy).then_inc(sem("h_hi"), 1)

            def tiles4(b):
                return b[:, :].rearrange("p (k c) -> p k c", k=4)

            def up_dve(dve, g0, j0, i):
                per = 0 if isinstance(i, int) else 2 * NP_IN
                ii = i if per else 0
                j = j0 + i
                for n in range(2 * NP_IN):
                    if n == NP_IN - 1:
                        for t in range(TT):
                            dve.wait_ge(sem("sg_tanh"), TT * j + t + 1)
                            nc.vector.scalar_tensor_tensor(out=sg[:, t, :], in0=sg[:, t, :], scalar=1.0,
                                                           in1=bank[t][:, :], op0=ALU.add, op1=ALU.mult)\
                                .then_inc(sem("acc_free"), 1)
                    if n == 2 * NP_IN - 1:
                        dve.wait_ge(sem("acc_free"), TT * (GATE_BLK(j0) + i) + TT)
                        for t in range(TT):
                            wait_acc(dve, "acc2", j, t, g0 + 2 * NP_IN + per * ii)
                            nc.vector.scalar_tensor_tensor(out=hb[:, t, :], in0=bank[3 + t][:, :], scalar=0.5,
                                                           in1=sg[:, t, :], op0=ALU.mult, op1=ALU.mult)\
                                .then_inc(sem("h_ready"), 1)
                        dve.wait_ge(sem("h_ready"), TT * j + TT)
                        dve.sem_inc(sem("acc2_free"), TT)
                    split_dve(dve, g0 + RING, n, ii, per)
                for t in range(TT):
                    dve.wait_ge(sem("h_hi"), TT * j + t + 1)
                    ks, ts_ = bass.ds(4 * i, 4), slice(t * P, (t + 1) * P)
                    nc.vector.tensor_tensor(hT_lo[:, ks, ts_], tiles4(bank[6 + t % 2]), hT_hi[:, ks, ts_],
                                            ALU.subtract).then_inc(sem("h_bank"), 1)

            def down_evac(dve, half, c, t, blk):
                wait_acc(dve, "acc", blk, t, (G_DN0, G_DN1)[half] + NP_DN[half] * (c + 1))
                xs = x_res[:, t, bass.ds(c * CW, CW)]
                nc.vector.scalar_tensor_tensor(out=xs, in0=xs, scalar=(ALPHA if half == 0 else 1.0),
                                               in1=bank[t][:, :], op0=ALU.mult, op1=ALU.add)\
                    .then_inc(sem("acc_free"), 1)
            BLK_DN = (BLK_MIX + FB[0], BLK_MIX + FB[0] + NCB + FB[1])

            @block.sync
            def _(sp):
                def up_loads(g0, j0, i, skip):
                    for n in range(skip, 2 * NP_IN):
                        w, m = (w_gate, n) if n < NP_IN else (w_up, n - NP_IN)
                        per = 0 if isinstance(i, int) else 2 * NP_IN
                        loads(sp, g0 + n + per * (i if per else 0), n % RAW,
                              plain_parts(w, m * KP * P, (j0 + i) * CW, n % RAW))

                def down_loads(g0, half, c, per):
                    for n in range(NP_DN[half]):
                        slot = (g0 + n) % RAW
                        loads(sp, g0 + n + per * (c if per else 0), slot,
                              plain_parts(w_down, (half * NP_DN[0] + n) * KP * P, c * CW, slot))
                up_loads(G_UP0, 0, 0, RAW + RING)
                with sp.Fori(0, FB[0] - 1) as i:
                    up_loads(G_UP0 + 2 * NP_IN, 1, i, 0)
                with sp.Fori(0, NCB) as c:
                    down_loads(G_DN0, 0, c, NP_DN[0])
                with sp.Fori(0, FB[1]) as i:
                    up_loads(G_UP1, FB[0], i, 0)
                for c in range(NCB):
                    down_loads(G_DN1 + NP_DN[1] * c, 1, c, 0)

            @block.scalar
            def _(act):
                with act.Fori(0, FB[0]) as i:
                    up_act(act, G_UP0, 0, i)
                with act.Fori(0, NCB) as c:
                    for n in range(NP_DN[0]):
                        split_act(act, G_DN0 + RING, n, c, NP_DN[0])
                with act.Fori(0, FB[1]) as i:
                    up_act(act, G_UP1, FB[0], i)
                for g in range(G_DN1 + RING, G_END):
                    split_act(act, g, 0)

            @block.vector
            def _(dve):
                dve.sem_inc(sem("h_bank"), 2)
                dve.sem_inc(sem("acc2_free"), TT)
                with dve.Fori(0, FB[0]) as i:
                    up_dve(dve, G_UP0, 0, i)
                with dve.Fori(0, NCB) as c:
                    for n in range(NP_DN[0]):
                        if n == NP_DN[0] - 1:
                            for t in range(TT):
                                down_evac(dve, 0, c, t, BLK_DN[0] + c)
                        split_dve(dve, G_DN0 + RING, n, c, NP_DN[0])
                with dve.Fori(0, FB[1]) as i:
                    up_dve(dve, G_UP1, FB[0], i)
                for c in range(NCB):
                    for n in range(NP_DN[1]):
                        if n == NP_DN[1] - 1:
                            for t in range(TT):
                                down_evac(dve, 1, c, t, BLK_DN[1] + c)
                        g = G_DN1 + c * NP_DN[1] + n + RING
                        if g < G_END:
                            split_dve(dve, g, 0)

            @block.tensor
            def _(pe):
                def hidden_ready(n):
                    pe.wait_ge(sem("h_bank"), n)
                with pe.Fori(0, FB[0]) as i:
                    up_pe(pe, G_UP0, 0, i)
                hidden_ready(2 + TT * FB[0])
                with pe.Fori(0, NCB) as c:
                    gemm(pe, G_DN0, NP_DN[0], hT_hi, hT_lo, 0, CW, ACC, "acc", BLK_DN[0], c, NP_DN[0], 1)
                with pe.Fori(0, FB[1]) as i:
                    up_pe(pe, G_UP1, FB[0], i)
                hidden_ready(2 + TT * (FB[0] + FB[1]))
                for c in range(NCB):
                    gemm(pe, G_DN1 + NP_DN[1] * c, NP_DN[1], hT_hi, hT_lo, 0, CW, ACC, "acc", BLK_DN[1] + c)

        with ExitStack() as ctx:
            gb = sb(ctx, "gb2", [P, 2, D])
            block = ctx.enter_context(nc.Block())

            @block.sync
            def _(sp):
                load_gb(sp, gb, ln_ffn_g[0], ln_ffn_b[0])
                for t in range(TT):
                    sp.wait_ge(sem("ln_done"), TT * 2 + t + 1)
                    dst = y_prompt[0, t * P:(t + 1) * P, :] if t < 2 else y_sample.rearrange("b s d -> (b s) d")
                    sp.dma_start(dst, x_res[:, t, :]).then_inc(sem("y_stored"), 16)
                sp.wait_ge(sem("y_stored"), 16 * TT)

            @block.scalar
            def _(act):
                for t in range(TT):
                    layer_norm_act(act, t, 2)

            @block.vector
            def _(dve):
                for t in range(TT):
                    layer_norm_dve(dve, t, gb, 2)


_INS = ["x_prompt", "x_sample", "cache_fox_k", "cache_fox_v", "cache_fox_logf", "state_gdn", "state_gdn_conv",
        "ln_in_g", "ln_in_b", "w_in", "fox_f_bias", "fox_norm_w", "gdn_conv_w", "gdn_a_log", "gdn_dt_bias",
        "gdn_norm_w", "w_out", "ln_mix_g", "ln_mix_b", "ffn_w_gate", "ffn_w_up", "ffn_w_down", "ln_ffn_g",
        "ln_ffn_b"]
_OUTS = [(1, 256, D), (NB, NQ, D),
         (1, 1, 256, HEADS, HD), (1, 1, 256, HEADS, HD), (1, 1, 256, HEADS), (1, 1, HEADS, HD, HD), (1, 1, 3, 3072),
         (1, NB, NQ, HEADS, HD), (1, NB, NQ, HEADS, HD), (1, NB, NQ, HEADS), (1, NB, HEADS, HD, HD),
         (1, NB, 3, 3072)]


def kernel(**inputs):
    import concourse.bacc as _bacc
    from concourse.bass_utils import run_bass_kernel_spmd as _run

    nc = _bacc.Bacc("TRN2", target_bir_lowering=False, num_devices=1)
    arrays, args = {}, []
    for name in _INS + ["constants"]:
        a = constants() if name == "constants" else np.ascontiguousarray(inputs[name])
        arrays[f"in_{name}"] = a
        args.append(nc.dram_tensor(f"in_{name}", a.shape, mybir.dt.from_np(a.dtype), kind="ExternalInput").ap())
    for i, shape in enumerate(_OUTS):
        args.append(nc.dram_tensor(f"out_{i}", shape, F32, kind="ExternalOutput").ap())
    encoder_layer(nc, *args)
    r = _run(nc, [arrays], core_ids=[0])
    return tuple(r.results[0][f"out_{i}"] for i in range(len(_OUTS)))
```

```python
from contextlib import ExitStack

import numpy as np

import concourse.bass as bass
from concourse import mybir

F32 = mybir.dt.float32
F32R = mybir.dt.float32r
I32 = mybir.dt.int32
ALU = mybir.AluOpType
ACT = mybir.ActivationFunctionType
AX = mybir.AxisListType.X

P = 128
D = 2048
TT = 3
TOK = TT * P
HEADS = 8
HD = 128
NB = 8
NQ = 16
DFF = 5632
KD = D // P
CW = 512
RAW = 8
RING = 4
A_ACT, A_DVE = 3, 3
LAG = 3
SLOTS = 3
SEG = TOK // NQ
TAP = 4
ALPHA = 2.0 ** 0.25
NEG = -1.0e30
SCALE = HD ** -0.5

FQ, FK, FV, FF = 0, 1024, 2048, 3072
GQ, GA, GZ = 3080, 6152, 6168

NP_IN = KD
G_FOX = 0
G_GDN = G_FOX + HEADS * NP_IN
G_OUT_FOX = G_GDN + HEADS * NP_IN
NCB = D // CW
NP_HALF = NP_IN // 2
G_OUT_GDN = G_OUT_FOX + NCB * NP_HALF
G_UP0 = G_OUT_GDN + NCB * NP_HALF
FB = (6, 5)
KH = FB[0] * CW // P
NP_DN = (FB[0] * CW // P, FB[1] * CW // P)
G_DN0 = G_UP0 + FB[0] * 2 * NP_IN
G_UP1 = G_DN0 + NCB * NP_DN[0]
G_DN1 = G_UP1 + FB[1] * 2 * NP_IN
G_END = G_DN1 + NCB * NP_DN[1]

C_ID, C_ONE, C_LP, C_LS, C_UP, C_US = (P * n for n in range(6))
C_MP = 6 * P
C_MS = C_MP + 2 * P
C_LV = C_MS + 2 * P
LEVELS = 7
F_OWN = 14
G_OWN = 32
GDN_TOK = (11, 14, 17)
STORE_AT = 12
HIDDEN_AT = (4, 7, 10)
GDN_LEVEL = 23
C_BM = C_LV + LEVELS * P
NC = C_BM + NB


def constants():
    i = np.arange(P)
    row, col = i[:, None], i[None, :]
    same = row // NQ == col // NQ
    c = np.zeros((P, NC), np.float32)
    c[:, C_ID:C_ID + P] = row == col
    c[:, C_ONE:C_ONE + P] = 1
    c[:, C_LP:C_LP + P] = row <= col
    c[:, C_LS:C_LS + P] = (row <= col) & same
    c[:, C_UP:C_UP + P] = row > col
    c[:, C_US:C_US + P] = (row > col) & same
    c[:, C_MP + P:C_MP + 2 * P] = np.where(col <= row, 0, NEG)
    c[:, C_MS + P:C_MS + 2 * P] = np.where((col <= row) & same, 0, NEG)
    for n in range(LEVELS):
        s = 1 << n
        c[:, C_LV + n * P:C_LV + (n + 1) * P] = (row // (2 * s) == col // (2 * s)) & (row // s % 2 == 1) & (col // s % 2 == 0)
    c[:, C_BM:C_BM + NB] = row // NQ == np.arange(NB)[None, :]
    return c


class Course:

    def __init__(self, program):
        self.program, self.at = program, next(program)

    def upto(self, slot):
        while self.at is not None and (slot is None or self.at <= slot):
            self.at = next(self.program, None)


def encoder_layer(nc, x_prompt, x_sample, cache_k, cache_v, cache_logf, state_gdn, state_conv, ln_in_g, ln_in_b,
                  w_in, fox_f_bias, fox_norm_w, gdn_conv_w, gdn_a_log, gdn_dt_bias, gdn_norm_w, w_out, ln_mix_g,
                  ln_mix_b, w_gate, w_up, w_down, ln_ffn_g, ln_ffn_b, const_in,
                  y_prompt, y_sample, o_kp, o_vp, o_lfp, o_sp, o_cp, o_ks, o_vs, o_lfs, o_ss, o_cs):
    w_in, w_out, w_gate, w_up, w_down = w_in[0], w_out[0], w_gate[0], w_up[0], w_down[0]
    sems = {}
    top = ExitStack()

    def sem(name):
        if name not in sems:
            sems[name] = top.enter_context(nc.semaphore(name))
        return sems[name]

    def pool_wait(pool, event, value):
        pool.wait_ge(event, value)
        pool.sem_inc(sem("pool_waited"), 1)

    def sb(ctx, name, shape, dt=F32):
        return ctx.enter_context(nc.sbuf_tensor(name, shape, dt))

    with top:
        x_res = sb(top, "x_res", [P, TT, D])
        aT_hi = sb(top, "aT_hi", [P, KD, TOK], F32R)
        aT_lo = sb(top, "aT_lo", [P, KD, TOK], F32R)
        raw = sb(top, "raw", [P, RAW, CW])
        w_hi = sb(top, "w_hi", [P, RING, CW], F32R)
        w_lo = sb(top, "w_lo", [P, RING, CW], F32R)
        cn = sb(top, "cn", [P, NC])
        bank = [top.enter_context(nc.psum_tensor(f"bank{n}", [P, 512], F32)) for n in range(8)]
        halves = raw[:].rearrange("p a c -> p (a c)")
        gb_last = (halves[:, 0:D], halves[:, D:2 * D])
        ident, ones = cn[:, C_ID:C_ID + P], cn[:, C_ONE:C_ONE + P]
        stats = sb(top, "stats", [P, TT, D // 512, 6])
        moments = sb(top, "moments", [P, TT, 2])
        rstd = sb(top, "rstd", [P, TT])
        var = sb(top, "var", [P, TT])
        pol = sb(top, "pol", [P, TT])
        shift = sb(top, "shift", [P, TT])
        ACC, ACC2 = bank[0:3], bank[3:6]

        def loads(sp, g, slot, parts, first=False):
            if not first:
                sp.wait_ge(sem("w_split"), g - RAW + 1)
            for dst, src in parts:
                sp.dma_start(dst, src).then_inc(sem(f"w_loaded{slot}"), 16)

        def dmas_of(g):
            return 2 if g < G_OUT_FOX + A_ACT else 1

        def plain_parts(w, row, c0, slot, dmas=1):
            part = CW // dmas
            return [(raw[:, slot, c:c + part], w[bass.ds(row, P), bass.ds(c0 + c, part)]) for c in range(0, CW, part)]

        def head_columns(row, c0, parts, h):
            return w_in[row:row + P, c0:c0 + parts * HEADS * HD].rearrange("p (a h c) -> p a h c", a=parts, c=HD)[:, :, h, :]

        def fox_parts(h, n, slot):
            r = raw[:, slot, :].rearrange("p (a c) -> p a c", c=HD)
            return [(r[:, 0:2, :], head_columns(n * P, FQ, 2, h)), (r[:, 2:3, :], head_columns(n * P, FV, 1, h))]

        def gdn_parts(h, n, slot):
            r = raw[:, slot, :].rearrange("p (a c) -> p a c", c=HD)
            return [(r[:, 0:3, :], head_columns(n * P, GQ, 3, h)), (r[:, 3:4, :], head_columns(n * P, GZ, 1, h))]

        def landed(g0, n, i, per):
            def total(g):
                return 16 * sum(dmas_of(q) for q in range(g % RAW, g + 1, RAW))
            first = total(g0 + n)
            return first + (total(g0 + n + per) - first) * i if per else first

        def split_act(act, g0, n, i=0, per=0):
            g = g0 + n
            act.wait_ge(sem(f"w_loaded{g % RAW}"), landed(g0, n, i, per))
            if g >= RING:
                act.wait_ge(sem("w_used"), g + per * i - RING + 1)
            nc.scalar.activation(w_hi[:, g % RING], raw[:, g % RAW], ACT.Copy).then_inc(sem("w_high"), 1)

        def split_dve(dve, g0, n, i=0, per=0):
            g = g0 + n
            dve.wait_ge(sem("w_high"), g + per * i + 1)
            nc.vector.tensor_tensor(w_lo[:, g % RING], raw[:, g % RAW], w_hi[:, g % RING],
                                    ALU.subtract).then_inc(sem("w_split"), 1)

        def gemm(pe, g0, pieces, hi, lo, k0, width, acc, name, block, i=0, per=0, blocks_per=0, between=None,
                 first=False, ends=True, slot0=0):
            for n in range(pieces):
                g = g0 + n
                pe.wait_ge(sem("w_split"), g + per * i + 1)
                for t in range(TT):
                    if n == 0 and not first:
                        pe.wait_ge(sem(name + "_free"), TT * (block - 1 + blocks_per * i) + t + 1)
                    for j, (l, r) in enumerate(((hi, w_hi), (hi, w_lo), (lo, w_hi))):
                        last = nc.tensor.matmul(acc[t][:, 0:width], l[:, k0 + n, t * P:(t + 1) * P],
                                                r[:, g % RING, 0:width], start=(n == 0 and j == 0),
                                                stop=(n == pieces - 1 and j == 2))
                    if t == TT - 1:
                        last.then_inc(sem("w_used"), 1)
                    elif n == pieces - 1:
                        last.then_inc(sem(name + "_done"), 1)
                    if between is not None:
                        between.upto(slot0 + SLOTS * n + t)
            if between is not None and ends:
                between.upto(None)

        def wait_acc(eng, name, block, t, g_end):
            if t < TT - 1:
                eng.wait_ge(sem(name + "_done"), (TT - 1) * block + t + 1)
            else:
                eng.wait_ge(sem("w_used"), g_end)

        def rsqrt(y, x, tmp, after):
            after(nc.vector.tensor_scalar(y.bitcast(I32), x.bitcast(I32), -0.5, float(0x5F3759DF), ALU.mult, ALU.add))
            for _ in range(3):
                after(nc.vector.tensor_tensor(tmp, y, y, ALU.mult))
                after(nc.vector.scalar_tensor_tensor(out=tmp, in0=tmp, scalar=-0.5, in1=x, op0=ALU.mult,
                                                     op1=ALU.mult))
                after(nc.vector.scalar_tensor_tensor(out=y, in0=tmp, scalar=1.5, in1=y, op0=ALU.add, op1=ALU.mult))

        chain = [0]

        def link(dve, ins):
            chain[0] += 1
            ins.then_inc(sem("dve_chain"), 1)
            dve.wait_ge(sem("dve_chain"), chain[0])

        QUARTERS = D // CW
        ROUNDS = TT * QUARTERS

        def row_stats(t, q):
            return nc.vector.bn_stats(stats[:, t, bass.ds(q, 1), :].rearrange("p a b -> p (a b)"),
                                      x_res[:, t, bass.ds(q * CW, CW)])

        def moments_dve(dve, ts, after_stats=None):
            for t in ts:
                last = nc.vector.bn_aggr(moments[:, t, :], stats[:, t].rearrange("p a b -> p (a b)"))
            link(dve, last)
            s = slice(ts[0], ts[-1] + 1)
            link(dve, nc.vector.tensor_scalar(var[:, s], moments[:, s, 1], 1e-5, None, ALU.add))
            rsqrt(rstd[:, s], var[:, s], pol[:, s], lambda ins: link(dve, ins))
            nc.vector.scalar_tensor_tensor(out=shift[:, s], in0=moments[:, s, 0], scalar=-1.0, in1=rstd[:, s],
                                           op0=ALU.mult, op1=ALU.mult).then_inc(sem("ln_moments"), 1)

        def quarter(r):
            t, q = divmod(r, QUARTERS)
            return t, x_res[:, t, q * CW:(q + 1) * CW], slice(q * CW, (q + 1) * CW)

        def normalise_act(act, r, norm, moments_count):
            if moments_count is not None:
                act.wait_ge(sem("ln_moments"), moments_count)
            t, x, _ = quarter(r)
            nc.scalar.activation(x, x, ACT.Identity, scale=rstd[:, t:t + 1], bias=shift[:, t:t + 1])\
                .then_inc(sem("ln_unit"), 1)

        def scale_dve(dve, r, gb, norm):
            if r == 0:
                dve.wait_ge(sem("gb_in"), 32 * (norm + 1))
            dve.wait_ge(sem("ln_unit"), ROUNDS * norm + r + 1)
            _, x, c = quarter(r)
            nc.vector.tensor_tensor(x, x, gb[0][:, c], ALU.mult).then_inc(sem("ln_scaled"), 1)

        def shift_pool(pool, r, gb, norm):
            if r == 0:
                pool_wait(pool, sem("gb_in"), 32 * (norm + 1))
            pool_wait(pool, sem("ln_scaled"), ROUNDS * norm + r + 1)
            _, x, c = quarter(r)
            nc.gpsimd.tensor_tensor(x, x, gb[1][:, c], ALU.add).then_inc(sem("ln_done"), 1)

        def load_gb(eng, gb, g, b):
            eng.dma_start(gb[0], g.partition_broadcast(P)).then_inc(sem("gb_in"), 16)
            eng.dma_start(gb[1], b.partition_broadcast(P)).then_inc(sem("gb_in"), 16)


        def x_transpose_pe(pe, r, norm):
            t, k4 = divmod(r, KD // 4)
            pe.wait_ge(sem("ln_done"), ROUNDS * norm + r + 1)
            if r >= 2:
                pe.wait_ge(sem("x_low"), ROUNDS * norm + r - 1)
            for k in range(4):
                c = (k4 * 4 + k) * P
                last = nc.tensor.transpose(bank[6 + r % 2][:, k * P:(k + 1) * P], x_res[:, t, c:c + P], ident)
            last.then_inc(sem("x_ps"), 1)

        def x_evac(r, dst):
            t, k4 = divmod(r, KD // 4)
            return (dst[:, 4 * k4:4 * k4 + 4, t * P:(t + 1) * P],
                    bank[6 + r % 2][:, :].rearrange("p (k c) -> p k c", k=4))

        def x_evac_act(act, r, norm):
            act.wait_ge(sem("x_ps"), ROUNDS * norm + r + 1)
            dst, src = x_evac(r, aT_hi)
            nc.scalar.activation(dst, src, ACT.Copy).then_inc(sem("x_high"), 1)

        def x_evac_dve(dve, r, norm):
            dve.wait_ge(sem("x_high"), ROUNDS * norm + r + 1)
            lo, src = x_evac(r, aT_lo)
            nc.vector.tensor_tensor(lo, src, x_evac(r, aT_hi)[0], ALU.subtract).then_inc(sem("x_low"), 1)

        def act_block(act, g0, i, per, mixer, evac):
            for n in range(NP_IN):
                if mixer is not None:
                    mixer.upto(SLOTS * n + SLOTS - 1)
                split_act(act, g0 + A_ACT, n, i, per)
            if evac is not None:
                for t in range(TT):
                    evac(t)
            if mixer is not None:
                mixer.upto(None)

        def dve_block(dve, g0, i, per, mixer):
            for n in range(NP_IN):
                if mixer is not None:
                    mixer.upto(SLOTS * n + SLOTS - 1)
                split_dve(dve, g0 + A_DVE, n, i, per)
            if mixer is not None:
                mixer.upto(None)

        mid = ExitStack()
        with mid:
            mixT_hi = sb(mid, "mixT_hi", [P, 2 * HEADS, TOK], F32R)
            mixT_lo = sb(mid, "mixT_lo", [P, 2 * HEADS, TOK], F32R)
            work_a = sb(mid, "work_a", [P, 3 * TOK + 3 * TT * HD])
            work_b = sb(mid, "work_b", [P, 2 * NB * HD])
            gb = (work_a[:, 0:D], work_b[:, 0:D])
            gate = sb(mid, "gate", [P, TT, 24])
            cfox = sb(mid, "cfox", [P, TT, HEADS])
            ccache = sb(mid, "ccache", [P, NB, HEADS])
            ncT = sb(mid, "ncT", [HEADS, TOK])
            nGT = sb(mid, "nGT", [HEADS, TOK])
            Gc = sb(mid, "Gc", [P, TT, HEADS])
            eG = sb(mid, "eG", [P, TT, HEADS])
            eR = sb(mid, "eR", [P, TT, HEADS])
            eL = sb(mid, "eL", [P, 2 + NB, HEADS])
            beta = sb(mid, "beta", [P, TT, HEADS])
            bhalf = sb(mid, "bhalf", [P, TT, HEADS])
            nbe = sb(mid, "nbe", [P, TT, HEADS])
            cw = sb(mid, "cw", [P, TAP * 24])
            cprev = sb(mid, "cprev", [P, 24, NB * 3])
            nwf = sb(mid, "nwf", [P, 1])
            nwg = sb(mid, "nwg", [P, 1])
            nwg2 = sb(mid, "nwg2", [P, 1])
            gbuf = sb(mid, "gbuf", [P, TT, CW])

            with ExitStack() as ctx:
                wg = sb(ctx, "wg", [P, KD, 24])
                wg_hi = sb(ctx, "wg_hi", [P, KD, 24], F32R)
                wg_lo = sb(ctx, "wg_lo", [P, KD, 24], F32R)
                gT = sb(ctx, "gT", [24, TOK])
                gbias = sb(ctx, "gbias", [P, 24])
                alog = sb(ctx, "alog", [P, HEADS])
                ea = sb(ctx, "ea", [P, HEADS])
                mag = sb(ctx, "mag", [P, TT, 16])
                soft = sb(ctx, "soft", [P, TT, 16])
                lf = sb(ctx, "lf", [P, TT, HEADS])
                gl = sb(ctx, "gl", [P, TT, HEADS])
                glb = sb(ctx, "glb", [P, NB, HEADS])
                lc = sb(ctx, "lc", [P, NB, HEADS])
                tsel = sb(ctx, "tsel", [P, NB, HEADS])
                tsum = sb(ctx, "tsum", [P, HEADS])
                cwraw = sb(ctx, "cwraw", [TAP * 24, P])
                stc = sb(ctx, "stc", [2 * NB * 3, 12 * P])
                sums_ps = bank[5]
                S_C, S_G, S_R, S_TP, S_TS, S_CC, S_CT = 0, 24, 48, 72, 88, 152, 216
                block = ctx.enter_context(nc.Block())

                def gates_pe(pe):
                    yield 0
                    pe.wait_ge(sem("x_low"), ROUNDS)
                    pe.wait_ge(sem("small"), 16 * 11)
                    for c in range(12):
                        last = nc.tensor.transpose(bank[6 + c // 6][:, c % 6 * 48:c % 6 * 48 + 48],
                                                   stc[:, c * P:(c + 1) * P], ident[0:48, 0:48])
                    last.then_inc(sem("st_ps"), 1)
                    pe.wait_ge(sem("wg_low"), 1)
                    for k in range(KD):
                        yield 1 + k
                        for j, (w, x) in enumerate(((wg_hi, aT_hi), (wg_hi, aT_lo), (wg_lo, aT_hi))):
                            last = nc.tensor.matmul(bank[3][0:24, 0:TOK], w[:, k, :], x[:, k, :],
                                                    start=(k == 0 and j == 0), stop=(k == KD - 1 and j == 2))
                    last.then_inc(sem("g_ps"), 1)
                    yield 20
                    pe.wait_ge(sem("gT"), 1)
                    for t in range(TT):
                        last = nc.tensor.transpose(bank[4][:, t * 24:t * 24 + 24], gT[:, t * P:(t + 1) * P],
                                                   ident[0:24, 0:24])
                    last.then_inc(sem("gate_ps"), 1)
                    yield 30
                    pe.wait_ge(sem("gl_ready"), 1)
                    LP, LS = cn[:, C_LP:C_LP + P], cn[:, C_LS:C_LS + P]
                    UP, US = cn[:, C_UP:C_UP + P], cn[:, C_US:C_US + P]

                    def sums(col, pairs):
                        for j, (l, r) in enumerate(pairs):
                            ins = nc.tensor.matmul(sums_ps[:, col:col + r.free_size()], l, r,
                                                   start=(j == 0), stop=(j == len(pairs) - 1))
                        return ins
                    sums(S_C, [(LP, lf[:, 0, :])])
                    sums(S_C + 8, [(LP, lf[:, 1, :]), (ones, lf[:, 0, :])])
                    sums(S_C + 16, [(LS, lf[:, 2, :])])
                    for t in range(TT):
                        sums(S_G + 8 * t, [(LP if t < 2 else LS, gl[:, t, :])])
                        sums(S_R + 8 * t, [(UP if t < 2 else US, gl[:, t, :])])
                    for t in range(2):
                        sums(S_TP + 8 * t, [(ones, gl[:, t, :])])
                    sums(S_TS, [(ones, glb[:].rearrange("p b h -> p (b h)"))])
                    sums(S_CC, [(LP, lc[:].rearrange("p b h -> p (b h)"))])
                    sums(S_CT, [(ones, lc[:].rearrange("p b h -> p (b h)"))]).then_inc(sem("sums"), 1)
                    nc.tensor.transpose(bank[4][:, 128:128 + TAP * 24], cwraw[:], ident[0:TAP * 24, 0:TAP * 24])
                    yield 38
                    pe.wait_ge(sem("c_ready"), 1)
                    for t in range(TT):
                        nc.tensor.transpose(bank[6][0:HEADS, t * P:(t + 1) * P], cfox[:, t, :], ident)
                        last = nc.tensor.transpose(bank[7][0:HEADS, t * P:(t + 1) * P], Gc[:, t, :], ident)
                    last.then_inc(sem("cT_ps"), 1)

                def gates_act(act):
                    yield 0
                    act.wait_ge(sem("small"), 16 * 11)
                    nc.scalar.activation(wg_hi[:], wg[:], ACT.Copy).then_inc(sem("wg_high"), 1)
                    nc.scalar.activation(ea[:], alog[:], ACT.Exp).then_inc(sem("ea"), 1)
                    yield 17
                    act.wait_ge(sem("g_ps"), 1)
                    nc.scalar.activation(gT[:], bank[3][0:24, 0:TOK], ACT.Copy).then_inc(sem("gT"), 1)
                    yield 20
                    act.wait_ge(sem("mag"), 1)
                    nc.scalar.activation(mag[:], mag[:], ACT.Exp, scale=-1.0).then_inc(sem("emag"), 1)
                    act.wait_ge(sem("emag"), 1)
                    nc.scalar.activation(mag[:], mag[:], ACT.Ln, bias=1.0).then_inc(sem("lnmag"), 1)
                    nc.scalar.activation(beta[:], gate[:, :, 16:24], ACT.Tanh, scale=0.5).then_inc(sem("tanhb"), 1)
                    yield 30
                    act.wait_ge(sem("sums"), 1)
                    nc.scalar.activation(eG[:], sums_ps[:, S_G:S_G + 24].rearrange("p (t h) -> p t h", t=TT), ACT.Exp)
                    nc.scalar.activation(eR[:], sums_ps[:, S_R:S_R + 24].rearrange("p (t h) -> p t h", t=TT), ACT.Exp)
                    nc.scalar.activation(eL[:], sums_ps[:, S_TP:S_CC].rearrange("p (t h) -> p t h", h=HEADS), ACT.Exp)\
                        .then_inc(sem("exps"), 1)

                def gates_dve(dve):
                    yield 0
                    dve.wait_ge(sem("wg_high"), 1)
                    nc.vector.tensor_tensor(wg_lo[:], wg[:], wg_hi[:], ALU.subtract).then_inc(sem("wg_low"), 1)
                    dve.wait_ge(sem("st_ps"), 1)
                    for j in range(2):
                        nc.vector.tensor_copy(
                            cprev[:].rearrange("p (g c) r -> p c g r", g=2)[:, 6 * j:6 * j + 6],
                            bank[6 + j][:, 0:288].rearrange("p (c g r) -> p c g r", c=6, g=2))
                    yield 20
                    dve.wait_ge(sem("gate_ps"), 1)
                    bias = gbias[:].unsqueeze(1).broadcast_to([P, TT, 24])
                    link(dve, nc.vector.tensor_tensor(
                        gate[:], bank[4][:, 0:72].rearrange("p (t c) -> p t c", t=TT), bias, ALU.add))
                    link(dve, nc.vector.tensor_scalar(gate[:, :, 0:8], gate[:, :, 0:8], -1.0, None, ALU.mult))
                    nc.vector.scalar_tensor_tensor(out=mag[:], in0=gate[:, :, 0:16], scalar=-1.0,
                                                   in1=gate[:, :, 0:16], op0=ALU.mult, op1=ALU.max)\
                        .then_inc(sem("mag"), 1)
                    yield 24
                    dve.wait_ge(sem("lnmag"), 1)
                    link(dve, nc.vector.scalar_tensor_tensor(out=soft[:], in0=gate[:, :, 0:16], scalar=0.0,
                                                             in1=mag[:], op0=ALU.max, op1=ALU.add))
                    nc.vector.tensor_scalar(lf[:], soft[:, :, 0:8], -1.0, None, ALU.mult).then_inc(sem("lf_ready"), 1)
                    dve.wait_ge(sem("ea"), 1)
                    link(dve, nc.vector.scalar_tensor_tensor(
                        out=gl[:], in0=soft[:, :, 8:16], scalar=-1.0,
                        in1=ea[:].unsqueeze(1).broadcast_to([P, TT, HEADS]), op0=ALU.mult, op1=ALU.mult))
                    nc.vector.tensor_tensor(
                        glb[:], gl[:, 2, :].unsqueeze(1).broadcast_to([P, NB, HEADS]),
                        cn[:, C_BM:C_BM + NB].unsqueeze(2).broadcast_to([P, NB, HEADS]), ALU.mult)\
                        .then_inc(sem("gl_ready"), 1)
                    dve.wait_ge(sem("tanhb"), 1)
                    link(dve, nc.vector.tensor_scalar(beta[:], beta[:], 1.0, 0.5, ALU.add, ALU.mult))
                    nc.vector.tensor_scalar(bhalf[:], beta[:], 0.5, None, ALU.mult)
                    link(dve, nc.vector.tensor_scalar(nwg2[:], nwg[:], 0.5, None, ALU.mult))
                    yield 30
                    dve.wait_ge(sem("exps"), 1)
                    link(dve, nc.vector.scalar_tensor_tensor(out=nbe[:], in0=beta[:], scalar=-1.0, in1=eG[:],
                                                             op0=ALU.mult, op1=ALU.mult))
                    link(dve, nc.vector.tensor_tensor(
                        tsel[:], sums_ps[:, S_CT:S_CT + 64].rearrange("p (b h) -> p b h", b=NB),
                        cn[:, C_BM:C_BM + NB].unsqueeze(2).broadcast_to([P, NB, HEADS]), ALU.mult))
                    nc.vector.tensor_copy(cfox[:, 0:2, :], sums_ps[:, S_C:S_C + 16].rearrange("p (t h) -> p t h", t=2))
                    nc.vector.tensor_copy(Gc[:], sums_ps[:, S_G:S_G + 24].rearrange("p (t h) -> p t h", t=TT))
                    nc.vector.tensor_copy(ccache[:], sums_ps[:, S_CC:S_CC + 64].rearrange("p (b h) -> p b h", b=NB))
                    link(dve, nc.vector.tensor_reduce(tsum[:], tsel[:].rearrange("p b h -> p h b"), AX, ALU.add))
                    nc.vector.tensor_tensor(cfox[:, 2, :], sums_ps[:, S_C + 16:S_C + 24], tsum[:], ALU.add)\
                        .then_inc(sem("c_ready"), 1)
                    yield 38
                    dve.wait_ge(sem("cT_ps"), 1)
                    nc.vector.tensor_scalar(ncT[:], bank[6][0:HEADS, 0:TOK], -1.0, None, ALU.mult)
                    nc.vector.tensor_scalar(nGT[:], bank[7][0:HEADS, 0:TOK], -1.0, None, ALU.mult)
                    nc.vector.tensor_copy(cw[:], bank[4][:, 128:128 + TAP * 24])

                @block.sync
                def _(sp):
                    sp.dma_start(x_res[:, 0, :], x_prompt[0, 0:P, :]).then_inc(sem("x_in0"), 16)
                    load_gb(sp, gb, ln_in_g, ln_in_b)
                    sp.dma_start(x_res[:, 1, :], x_prompt[0, P:2 * P, :]).then_inc(sem("x_in1"), 16)
                    sp.dma_start(x_res[:, 2, :], x_sample.rearrange("b s d -> (b s) d")).then_inc(sem("x_in2"), 16)
                    for n in range(RAW):
                        sp.wait_ge(sem("raw_zero"), 1)
                        loads(sp, n, n, fox_parts(0, n, n), first=True)
                    for n in range(RAW, NP_IN + RAW + A_DVE):
                        h, m = divmod(n, NP_IN)
                        loads(sp, n, n % RAW, fox_parts(h, m, n % RAW))

                @block.gpsimd
                def _(pool):
                    pool.dma_start(cn[:], const_in).then_inc(sem("consts"), 16)
                    pool.dma_start(wg[:, :, 0:8], w_in[:, FF:FF + 8].rearrange("(k p) c -> p k c", p=P))\
                        .then_inc(sem("small"), 16)
                    pool.dma_start(wg[:, :, 8:24], w_in[:, GA:GZ].rearrange("(k p) c -> p k c", p=P))\
                        .then_inc(sem("small"), 16)
                    nc.gpsimd.memset(gbias[:], 0.0).then_inc(sem("bias_zero"), 1)
                    pool_wait(pool, sem("bias_zero"), 1)
                    pool.dma_start(gbias[:, 0:8], fox_f_bias[0].partition_broadcast(P)).then_inc(sem("small"), 16)
                    pool.dma_start(gbias[:, 8:16], gdn_dt_bias[0].partition_broadcast(P)).then_inc(sem("small"), 16)
                    pool.dma_start(alog[:], gdn_a_log[0].partition_broadcast(P)).then_inc(sem("small"), 16)
                    pool.dma_start(lc[:], cache_logf[0].rearrange("b t h -> t b h")).then_inc(sem("small"), 16)
                    pool.dma_start(nwf[:], fox_norm_w.rearrange("a p -> p a")).then_inc(sem("small"), 16)
                    pool.dma_start(nwg[:], gdn_norm_w.rearrange("a p -> p a")).then_inc(sem("small"), 16)
                    pool.dma_start(cwraw[:], gdn_conv_w[0].rearrange("r (c p) -> (r c) p", p=P))\
                        .then_inc(sem("small"), 16)
                    for half in range(2):
                        pool.dma_start(stc[half * 24:half * 24 + 24, :],
                                       state_conv[0].rearrange("b r c -> (b r) c")[:, half * 12 * P:(half + 1) * 12 * P])\
                            .then_inc(sem("small"), 16)
                    for r in range(ROUNDS):
                        shift_pool(pool, r, gb, 0)
                    pool_wait(pool, sem("lf_ready"), 1)
                    pool.dma_start(o_lfp[0, 0].rearrange("(t p) h -> p t h", p=P), lf[:, 0:2, :])\
                        .then_inc(sem("lf_stored"), 16)
                    pool.dma_start(o_lfs[0].rearrange("b s h -> (b s) h"), lf[:, 2, :])\
                        .then_inc(sem("lf_stored"), 16)
                    pool_wait(pool, sem("lf_stored"), 32)

                @block.scalar
                def _(act):
                    for r in range(ROUNDS + LAG):
                        if r < ROUNDS:
                            normalise_act(act, r, 0, r // QUARTERS + 1 if r % QUARTERS == 0 else None)
                        if r >= LAG:
                            x_evac_act(act, r - LAG, 0)
                        if ROUNDS - LAG <= r < ROUNDS - LAG + A_ACT:
                            split_act(act, r - (ROUNDS - LAG), 0)
                    act_block(act, G_FOX, 0, 0, Course(gates_act(act)), None)

                @block.vector
                def _(dve):
                    nc.vector.memset(raw[:], 0.0).then_inc(sem("raw_zero"), 1)
                    def tile_moments(t):
                        dve.wait_ge(sem(f"x_in{t}"), 16)
                        for q in range(QUARTERS):
                            last = row_stats(t, q)
                        link(dve, last)
                        moments_dve(dve, [t])
                    tile_moments(0)
                    for r in range(ROUNDS + LAG):
                        if r < ROUNDS:
                            scale_dve(dve, r, gb, 0)
                        if r >= LAG:
                            x_evac_dve(dve, r - LAG, 0)
                        if r % QUARTERS == 2 and r // QUARTERS + 1 < TT:
                            tile_moments(r // QUARTERS + 1)
                        if ROUNDS - LAG <= r < ROUNDS - LAG + A_DVE:
                            split_dve(dve, r - (ROUNDS - LAG), 0)
                    dve_block(dve, G_FOX, 0, 0, Course(gates_dve(dve)))

                @block.tensor
                def _(pe):
                    pe.wait_ge(sem("consts"), 16)
                    for r in range(ROUNDS):
                        x_transpose_pe(pe, r, 0)
                    gemm(pe, G_FOX, NP_IN, aT_hi, aT_lo, 0, 3 * HD, ACC, "acc", 0, first=True,
                         between=Course(gates_pe(pe)))

            b3, b4, b5, b6, b7 = bank[3:8]

            def tiles(ap, n=TT):
                return ap.rearrange("p (t c) -> p t c", t=n)

            def per_token(x, h, n=TT):
                return x[:, 0:n, bass.ds(h, 1)].broadcast_to([P, n, HD])

            with ExitStack() as ctx:
                fbuf = sb(ctx, "fbuf", [P, TT, 3 * HD])
                kc, vc = (work_b[:, n * NB * HD:(n + 1) * NB * HD].rearrange("p (b c) -> p b c", b=NB) for n in (0, 1))
                kcT = work_a[:, 0:NB * HD]
                qkT = work_a[:, NB * HD:NB * HD + 2 * TOK].rearrange("p (a c) -> p a c", a=2)
                nch = sb(ctx, "nch", [HEADS, TOK])
                scT = sb(ctx, "scT", [P, P])
                sc = sb(ctx, "sc", [P, TT, 2 * P])
                nmax = sb(ctx, "nmax", [P, TT])
                den = sb(ctx, "den", [P, TT])
                rden = sb(ctx, "rden", [P, TT])
                pT = sb(ctx, "pT", [P, 5, P])
                o2T = sb(ctx, "o2T", [P, P])
                fo = sb(ctx, "fo", [P, TT, HD])
                fsq = sb(ctx, "fsq", [P, TT, HD])
                fss = sb(ctx, "fss", [P, TT])
                frs = sb(ctx, "frs", [P, TT])
                block = ctx.enter_context(nc.Block())
                qT, kT = qkT[:, 0, :], qkT[:, 1, :]

                def fox_pe(pe, h):
                    def W(name):
                        pe.wait_ge(sem(name), h + 1)
                    yield 2
                    pe.wait_ge(sem("f_buf"), TT * (h + 1))
                    for t in range(TT):
                        last = nc.tensor.transpose(b3[:, t * P:(t + 1) * P], fbuf[:, t, 0:HD], ident)
                    last.then_inc(sem("f_qT_ps"), 1)
                    yield 4
                    for t in range(TT):
                        last = nc.tensor.transpose(b4[:, t * P:(t + 1) * P], fbuf[:, t, HD:2 * HD], ident)
                    last.then_inc(sem("f_kT_ps"), 1)
                    yield 6
                    pe.wait_ge(sem("kc_in"), 16 * (h + 1))
                    for b in range(4):
                        last = nc.tensor.transpose(b5[:, b * P:(b + 1) * P], kc[:, b, :], ident)
                    last.then_inc(sem("f_kcT_ps0"), 1)
                    yield 8
                    for b in range(4):
                        last = nc.tensor.transpose(b6[:, b * P:(b + 1) * P], kc[:, 4 + b, :], ident)
                    last.then_inc(sem("f_kcT_ps1"), 1)
                    yield 10
                    W("f_qT"), W("f_kT"), W("f_nch")
                    one8 = ones[0:HEADS, :]
                    nc.tensor.matmul(b3[:, 0:2 * P], qT[:, P:2 * P], kT[:, 0:2 * P], start=True, stop=False)
                    nc.tensor.matmul(b3[:, 0:2 * P], one8, nch[:, 0:2 * P], start=False, stop=True)
                    nc.tensor.matmul(b3[:, 2 * P:3 * P], qT[:, 0:P], kT[:, 0:P], start=True, stop=False)
                    nc.tensor.matmul(b3[:, 2 * P:3 * P], one8, nch[:, 0:P], start=False, stop=True)\
                        .then_inc(sem("f_sp_ps"), 1)
                    yield 13
                    nc.tensor.matmul(b4[:, P:2 * P], qT[:, 2 * P:], kT[:, 2 * P:], start=True, stop=False)
                    nc.tensor.matmul(b4[:, P:2 * P], one8, nch[:, 2 * P:], start=False, stop=True)
                    W("f_kcT0"), W("f_kcT1")
                    for b in range(NB):
                        c = slice(b * NQ, (b + 1) * NQ)
                        last = nc.tensor.matmul(b7[:, c], kcT[:, b * HD:(b + 1) * HD],
                                                qT[:, 2 * P + b * NQ:2 * P + (b + 1) * NQ], start=True, stop=True)
                    last.then_inc(sem("f_scT_ps"), 1)
                    yield 18
                    W("f_scT")
                    nc.tensor.transpose(b4[:, 0:P], scT[:], ident).then_inc(sem("f_ss_ps"), 1)
                    yield 26
                    W("f_p")
                    for j, (t, c) in enumerate(((0, 0), (1, 0), (1, P), (2, P))):
                        last = nc.tensor.transpose(b6[:, j * P:(j + 1) * P], sc[:, t, c:c + P], ident)
                    last.then_inc(sem("f_pT_ps0"), 1)
                    nc.tensor.transpose(b7[:, 0:P], sc[:, 2, 0:P], ident).then_inc(sem("f_pT_ps1"), 1)
                    yield 30
                    W("f_pT0"), W("f_pT1")
                    v = fbuf[:, :, 2 * HD:]
                    nc.tensor.matmul(b7[:, 0:P], v[:, 2, :], pT[:, 3, :], start=True, stop=False)
                    pe.wait_ge(sem("vc_in"), 16 * (h + 1))
                    for b in range(NB):
                        c = slice(b * NQ, (b + 1) * NQ)
                        last = nc.tensor.matmul(b7[:, c], vc[:, b, :], pT[:, 4, c], start=False, stop=(b == NB - 1))
                    last.then_inc(sem("f_o2_ps"), 1)
                    yield 34
                    nc.tensor.matmul(b5[:, 0:P], pT[:, 0, :], v[:, 0, :], start=True, stop=True)
                    nc.tensor.matmul(b5[:, P:2 * P], pT[:, 1, :], v[:, 0, :], start=True, stop=False)
                    nc.tensor.matmul(b5[:, P:2 * P], pT[:, 2, :], v[:, 1, :], start=False, stop=True)
                    W("f_o2T")
                    nc.tensor.transpose(b5[:, 2 * P:3 * P], o2T[:], ident).then_inc(sem("f_o_ps"), 1)
                    yield 44
                    W("f_o")
                    for t in range(TT):
                        last = nc.tensor.transpose(b3[:, t * P:(t + 1) * P], fo[:, t, :], ident)
                    last.then_inc(sem("f_oT_ps"), 1)
                    yield 47
                    W("f_mix")

                def fox_act(act, h):
                    def W(name):
                        act.wait_ge(sem(name), h + 1)
                    yield 2
                    W("f_qT_ps")
                    nc.scalar.activation(qT, b3[:, 0:TOK], ACT.Copy, scale=SCALE).then_inc(sem("f_qT"), 1)
                    yield 6
                    W("f_kcT_ps0")
                    nc.scalar.activation(kcT[:, 0:512], b5[:, :], ACT.Copy).then_inc(sem("f_kcT0"), 1)
                    yield 8
                    W("f_kcT_ps1")
                    nc.scalar.activation(kcT[:, 512:], b6[:, :], ACT.Copy).then_inc(sem("f_kcT1"), 1)
                    yield 18
                    W("f_max")
                    for t, w in ((0, P), (1, 2 * P), (2, 2 * P)):
                        last = nc.scalar.activation(sc[:, t, 0:w], sc[:, t, 0:w], ACT.Exp, bias=nmax[:, t:t + 1],
                                                    accum_out=den[:, t:t + 1])
                    last.then_inc(sem("f_p"), 1)
                    yield 26
                    W("f_pT_ps0")
                    nc.scalar.activation(pT[:, 0:4, :], tiles(b6[:, :], 4), ACT.Copy).then_inc(sem("f_pT0"), 1)
                    yield 44
                    W("f_oT_ps")
                    nc.scalar.activation(mixT_hi[:, bass.ds(h, 1), :], b3[:, 0:TOK].unsqueeze(1), ACT.Copy, scale=nwf[:])\
                        .then_inc(sem("f_mix_hi"), 1)

                def fox_dve(dve, h):
                    def W(name):
                        dve.wait_ge(sem(name), h + 1)

                    own = [0]

                    def after(ins):
                        own[0] += 1
                        ins.then_inc(sem("f_own"), 1)
                        dve.wait_ge(sem("f_own"), F_OWN * h + own[0])
                    yield 4
                    nc.vector.tensor_scalar(nch[:], ncT[:], cn[0:HEADS, bass.ds(C_ID + h, 1)], None, ALU.mult)\
                        .then_inc(sem("f_nch"), 1)
                    W("f_kT_ps")
                    nc.vector.tensor_copy(kT, b4[:, 0:TOK]).then_inc(sem("f_kT"), 1)
                    yield 10
                    W("f_sp_ps")
                    nc.vector.scalar_tensor_tensor(
                        out=sc[:, 1, :], in0=b3[:, 0:2 * P], scalar=cfox[:, 1, bass.ds(h, 1)],
                        in1=cn[:, C_MP:C_MP + 2 * P], op0=ALU.add, op1=ALU.add)
                    nc.vector.scalar_tensor_tensor(
                        out=sc[:, 0, 0:P], in0=b3[:, 2 * P:3 * P], scalar=cfox[:, 0, bass.ds(h, 1)],
                        in1=cn[:, C_MP + P:C_MP + 2 * P], op0=ALU.add, op1=ALU.add)
                    yield 13
                    W("f_scT_ps")
                    nc.vector.tensor_tensor(
                        scT[:].rearrange("p (b q) -> p b q", b=NB), b7[:, 0:P].rearrange("p (b q) -> p b q", b=NB),
                        ccache[:, :, bass.ds(h, 1)].broadcast_to([P, NB, NQ]), ALU.subtract)\
                        .then_inc(sem("f_scT"), 1)
                    yield 18
                    W("f_ss_ps")
                    after(nc.vector.scalar_tensor_tensor(
                        out=sc[:, 2, :], in0=b4[:, 0:2 * P], scalar=cfox[:, 2, bass.ds(h, 1)],
                        in1=cn[:, C_MS:C_MS + 2 * P], op0=ALU.add, op1=ALU.add))
                    for t, w in ((0, P), (1, 2 * P), (2, 2 * P)):
                        last = nc.vector.tensor_reduce(nmax[:, t:t + 1], sc[:, t, 0:w], AX, ALU.max, negate=True)
                    last.then_inc(sem("f_max"), 1)
                    yield 26
                    W("f_p")
                    nc.vector.reciprocal(rden[:], den[:]).then_inc(sem("f_rden"), 1)
                    W("f_pT_ps1")
                    nc.vector.tensor_copy(pT[:, 4, :], b7[:, 0:P]).then_inc(sem("f_pT1"), 1)
                    yield 30
                    W("f_o2_ps")
                    nc.vector.tensor_copy(o2T[:], b7[:, 0:P]).then_inc(sem("f_o2T"), 1)
                    yield 34
                    W("f_o_ps"), W("f_rden")
                    for t in range(TT):
                        last = nc.vector.tensor_scalar(fo[:, t, :], b5[:, t * P:(t + 1) * P], rden[:, t:t + 1], None,
                                                       ALU.mult)
                    after(last)
                    for t in range(TT):
                        last = nc.vector.scalar_tensor_tensor(
                            out=fsq[:, t, :], in0=fo[:, t, :], scalar=1.0, in1=fo[:, t, :], op0=ALU.mult,
                            op1=ALU.mult, accum_out=fss[:, t:t + 1])
                    after(last)
                    after(nc.vector.tensor_scalar(fss[:], fss[:], 1.0 / HD, 1e-6, ALU.mult, ALU.add))
                    yield 37
                    rsqrt(frs[:], fss[:], pol[:], after)
                    for t in range(TT):
                        last = nc.vector.tensor_scalar(fo[:, t, :], fo[:, t, :], frs[:, t:t + 1], None, ALU.mult)
                    last.then_inc(sem("f_o"), 1)
                    yield 44
                    W("f_mix_hi")
                    nc.vector.scalar_tensor_tensor(
                        out=mixT_lo[:, bass.ds(h, 1), :], in0=b3[:, 0:TOK].unsqueeze(1), scalar=nwf[:],
                        in1=mixT_hi[:, bass.ds(h, 1), :], op0=ALU.mult, op1=ALU.subtract).then_inc(sem("f_mix"), 1)
                    assert own[0] == F_OWN

                def fox_evac(act, h, t):
                    wait_acc(act, "acc", h, t, G_FOX + NP_IN * (h + 1))
                    nc.scalar.activation(fbuf[:, t, :], bank[t][:, 0:3 * HD], ACT.Copy)\
                        .then_inc(sem("f_buf"), 1)
                    act.wait_ge(sem("f_buf"), TT * h + t + 1)
                    act.sem_inc(sem("acc_free"), 1)

                def gdn_evac(act, h, t):
                    wait_acc(act, "acc", HEADS + h, t, G_GDN + NP_IN * (h + 1))
                    nc.scalar.activation(gbuf[:, t, :], bank[t][:, :], ACT.Copy).then_inc(sem("g_buf"), 1)
                    act.wait_ge(sem("g_buf"), TT * h + t + 1)
                    act.sem_inc(sem("acc_free"), 1)

                @block.sync
                def _(sp):
                    for n in range(RAW + A_DVE, NP_IN):
                        loads(sp, NP_IN + n, n % RAW, fox_parts(1, n, n % RAW))
                    with sp.Fori(0, HEADS - 2) as i:
                        for n in range(NP_IN):
                            loads(sp, 2 * NP_IN + n + NP_IN * i, n % RAW, fox_parts(i + 2, n, n % RAW))
                    for n in range(NP_IN):
                        loads(sp, G_GDN + n, n % RAW, gdn_parts(0, n, n % RAW))
                    for n in range(RAW + A_DVE):
                        loads(sp, G_GDN + NP_IN + n, n % RAW, gdn_parts(1, n, n % RAW))

                @block.gpsimd
                def _(pool):
                    def load_cache(dst, src, h, name):
                        pool.dma_start(dst[:], src[0, :, :, bass.ds(h, 1), :].rearrange("b t o d -> t b (o d)"))\
                            .then_inc(sem(name), 16)

                    def store(h, last):
                        pool_wait(pool, sem("f_buf"), TT * (h + 1))
                        for part, prompt, sample in ((1, o_kp, o_ks), (2, o_vp, o_vs)):
                            c = slice(part * HD, (part + 1) * HD)
                            pool.dma_start(prompt[0, 0, :, bass.ds(h, 1), :].rearrange("(t p) o d -> p t (o d)", p=P),
                                           fbuf[:, 0:2, c]).then_inc(sem("f_stored"), 16)
                            pool.dma_start(sample[0, :, :, bass.ds(h, 1), :].rearrange("b s o d -> (b s) (o d)"),
                                           fbuf[:, 2, c]).then_inc(sem("f_stored"), 16)
                        if not last:
                            pool_wait(pool, sem("f_kcT_ps1"), h + 1)
                            load_cache(kc, cache_k, h + 1, "kc_in")
                            pool_wait(pool, sem("f_o2_ps"), h + 1)
                            load_cache(vc, cache_v, h + 1, "vc_in")
                    load_cache(kc, cache_k, 0, "kc_in")
                    load_cache(vc, cache_v, 0, "vc_in")
                    with pool.Fori(0, HEADS - 1) as i:
                        store(i, False)
                    store(HEADS - 1, True)
                    pool_wait(pool, sem("f_stored"), 64 * HEADS)

                @block.scalar
                def _(act):
                    for t in range(TT):
                        fox_evac(act, 0, t)
                    with act.Fori(0, HEADS - 1) as i:
                        act_block(act, G_FOX + NP_IN, i, NP_IN, Course(fox_act(act, i)), lambda t: (
                            act.wait_ge(sem("f_stored"), 64 * (i + 1)), fox_evac(act, i + 1, t)))
                    act_block(act, G_GDN, 0, 0, Course(fox_act(act, HEADS - 1)), lambda t: gdn_evac(act, 0, t))

                @block.vector
                def _(dve):
                    with dve.Fori(0, HEADS - 1) as i:
                        dve_block(dve, G_FOX + NP_IN, i, NP_IN, Course(fox_dve(dve, i)))
                    dve_block(dve, G_GDN, 0, 0, Course(fox_dve(dve, HEADS - 1)))

                @block.tensor
                def _(pe):
                    with pe.Fori(0, HEADS - 1) as i:
                        gemm(pe, G_FOX + NP_IN, NP_IN, aT_hi, aT_lo, 0, 3 * HD, ACC, "acc", 1, i, NP_IN, 1,
                             Course(fox_pe(pe, i)))
                    gemm(pe, G_GDN, NP_IN, aT_hi, aT_lo, 0, CW, ACC, "acc", HEADS, between=Course(fox_pe(pe, HEADS - 1)))

            with ExitStack() as ctx:
                early = sb(ctx, "early", [P, 3 * SEG * (NQ + 3)])
                ext = early[:].rearrange("p (a s q) -> p a s q", a=3, s=SEG)
                A, B, T = (early[:, n * TOK:(n + 1) * TOK].rearrange("p (t c) -> p t c", t=TT) for n in range(3))
                cv = work_a[:, 0:3 * TOK].rearrange("p (a c) -> p a c", a=3)
                R, vn, oq = (cv[:, n, :].rearrange("p (t c) -> p t c", t=TT) for n in range(3))
                nq = work_a[:, 3 * TOK:].rearrange("p (a t c) -> p a t c", a=3, t=TT)
                ke = sb(ctx, "ke", [P, TT, HD])
                gT2 = sb(ctx, "g_kqT", [P, 2, TOK])
                dec = sb(ctx, "dec", [P, TT, P])
                go = dec
                U = sb(ctx, "U", [P, TT, P])
                qkd = sb(ctx, "qkd", [P, TT, P])
                Z = qkd
                qkdT = sb(ctx, "qkdT", [P, TT, P])
                S, vm = (work_b[:, n * NB * HD:(n + 1) * NB * HD].rearrange("p (b c) -> p b c", b=NB) for n in (0, 1))
                flat = work_b[:, NB * HD:]
                ngh, ksT = flat[0:HEADS, 0:TOK], flat[:, 512:768].rearrange("p (a c) -> p a c", a=2)
                S1 = sb(ctx, "S1", [P, HD])
                gss = sb(ctx, "gss", [P, TT])
                nss = sb(ctx, "nss", [P, 2, TT])
                nrs = sb(ctx, "nrs", [P, 2, TT])
                npol = sb(ctx, "npol", [P, 2, TT])
                grs = sb(ctx, "grs", [P, TT])
                zg = gbuf[:, :, 0:HD]
                block = ctx.enter_context(nc.Block())
                kTn, qTn = gT2[:, 0, :], gT2[:, 1, :]
                cvb = (b3, b4, b5)
                lv = [cn[:, C_LV + n * P:C_LV + (n + 1) * P] for n in range(LEVELS)]

                def n_tiles(level):
                    return TT if (1 << level) < NQ else 2

                def tl(x, t, c=P):
                    return x[:, t * c:(t + 1) * c]

                def gdn_pe(pe, h):
                    def W(name):
                        pe.wait_ge(sem(name), h + 1)

                    def L(name, n, per_head):
                        pe.wait_ge(sem(name), per_head * h + n)
                    yield 2
                    pe.wait_ge(sem("g_buf"), TT * (h + 1))
                    for a in range(3):
                        yield 2 + a
                        if a == 0:
                            W("g_state"), W("g_mix")
                        for t in range(TT):
                            last = nc.tensor.transpose(tl(cvb[a], t), gbuf[:, t, a * HD:(a + 1) * HD], ident)
                        last.then_inc(sem("g_raw_ps"), 1)
                    for a, bk in enumerate((b6, b7, b3)):
                        yield GDN_TOK[a]
                        L("g_cv", a + 1, 3)
                        for t in range(TT):
                            last = nc.tensor.transpose(tl(bk, t), tl(cv[:, a, :], t), ident)
                        last.then_inc(sem("g_tok_ps"), 1)
                    yield 19
                    W("g_nq")
                    for t in range(TT):
                        last = nc.tensor.transpose(tl(b4, t), nq[:, 0, t, :], ident)
                    last.then_inc(sem("g_qT_ps"), 1)
                    W("g_nk")
                    for t in range(TT):
                        last = nc.tensor.transpose(tl(b5, t), nq[:, 1, t, :], ident)
                    last.then_inc(sem("g_kT_ps"), 1)
                    yield 21
                    W("g_qT"), W("g_kT"), W("g_ngh"), W("g_nv")
                    nc.tensor.matmul(b3[:, 0:TOK], ones[0:HEADS, :], ngh, start=True, stop=True)\
                        .then_inc(sem("g_dec_ps"), 1)
                    for t in range(TT):
                        last = nc.tensor.matmul(tl(b6, t), tl(kTn, t), tl(kTn, t), start=True, stop=True)
                    last.then_inc(sem("g_kk_ps"), 1)
                    for t in range(TT):
                        last = nc.tensor.matmul(tl(b7, t), tl(qTn, t), tl(kTn, t), start=True, stop=True)
                    last.then_inc(sem("g_qk_ps"), 1)
                    yield 22
                    pe.wait_ge(sem("g_S_in"), 16 * (h + 1))
                    for b in range(NB):
                        last = nc.tensor.matmul(b4[:, 0:2 * P].rearrange("p (a c) -> p a c", a=2)[:, :, b * NQ:(b + 1) * NQ],
                                                S[:, b, :], gT2[:, :, 2 * P + b * NQ:2 * P + (b + 1) * NQ],
                                                start=True, stop=True)
                    last.then_inc(sem("g_ksT_ps"), 1)
                    yield 24
                    W("g_T1")
                    for t in range(TT):
                        last = nc.tensor.transpose(tl(b5, t), T[:, t, :], ident)
                    last.then_inc(sem("g_U1_ps"), 1)
                    W("g_qkd")
                    for t in range(TT):
                        last = nc.tensor.transpose(tl(b3, t), qkd[:, t, :], ident)
                    last.then_inc(sem("g_qkdT_ps"), 1)
                    W("g_ksT")
                    for a in range(2):
                        last = nc.tensor.transpose(b7[:, a * P:(a + 1) * P], ksT[:, a, :], ident)
                    last.then_inc(sem("g_ks_ps"), 1)
                    for n in range(1, LEVELS):
                        yield GDN_LEVEL + 2 * n
                        L("g_U", n, LEVELS), L("g_B", n, LEVELS - 1)
                        for t in range(n_tiles(n)):
                            last = nc.tensor.matmul(tl(b6, t), B[:, t, :], U[:, t, :], start=True, stop=True)
                        last.then_inc(sem("g_Z_ps"), 1)
                        if n > 1:
                            for t in range(n_tiles(n)):
                                last = nc.tensor.transpose(tl(b4, t), U[:, t, :], ident)
                            last.then_inc(sem("g_T_ps"), 1)
                        yield GDN_LEVEL + 2 * n + 1
                        L("g_Z", n, LEVELS - 1)
                        if n > 1:
                            L("g_Tl", n - 1, LEVELS - 2)
                        for t in range(n_tiles(n)):
                            last = nc.tensor.matmul(tl(b5, t), T[:, t, :], Z[:, t, :], start=True, stop=True)
                        last.then_inc(sem("g_UZ_ps"), 1)
                    yield 38
                    L("g_U", LEVELS, LEVELS), W("g_R2"), W("g_qkdT")
                    nc.tensor.matmul(tl(b6, 0), U[:, 0, :], nq[:, 2, 0, :], start=True, stop=True)
                    nc.tensor.matmul(tl(b6, 2), U[:, 2, :], R[:, 2, :], start=True, stop=True)\
                        .then_inc(sem("g_v02_ps"), 1)
                    yield 39
                    W("g_v02"), W("g_ke")
                    nc.tensor.matmul(tl(b4, 0), ke[:, 0, :], vn[:, 0, :], start=True, stop=True)\
                        .then_inc(sem("g_S1_ps"), 1)
                    nc.tensor.matmul(tl(b7, 0), qkdT[:, 0, :], vn[:, 0, :], start=True, stop=True)
                    nc.tensor.matmul(tl(b7, 2), qkdT[:, 2, :], vn[:, 2, :], start=True, stop=True)
                    yield 40
                    W("g_S1")
                    nc.tensor.matmul(b5[:, 0:P], tl(kTn, 1), S1[:], start=True, stop=True)
                    nc.tensor.matmul(b5[:, P:2 * P], tl(qTn, 1), S1[:], start=True, stop=True)\
                        .then_inc(sem("g_ks1_ps"), 1)
                    yield 41
                    W("g_R1")
                    nc.tensor.matmul(tl(b6, 0), U[:, 1, :], R[:, 1, :], start=True, stop=True)\
                        .then_inc(sem("g_v1_ps"), 1)
                    yield 42
                    W("g_vm")
                    nc.tensor.matmul(b3[:, :], ke[:, 2, :], vm[:, 0:4, :].rearrange("p b c -> p (b c)"), start=True,
                                     stop=True)
                    W("g_v1")
                    nc.tensor.matmul(tl(b7, 1), qkdT[:, 1, :], vn[:, 1, :], start=True, stop=True)\
                        .then_inc(sem("g_o_ps"), 1)
                    nc.tensor.matmul(b4[:, 0:P], ke[:, 1, :], vn[:, 1, :], start=True, stop=True)\
                        .then_inc(sem("g_S2_ps"), 1)
                    W("g_R1")
                    nc.tensor.matmul(b5[:, :], ke[:, 2, :], vm[:, 4:8, :].rearrange("p b c -> p (b c)"), start=True,
                                     stop=True).then_inc(sem("g_Ss_ps"), 1)
                    yield 47
                    W("g_o")
                    for t in range(TT):
                        last = nc.tensor.transpose(tl(b6, t), go[:, t, :], ident)
                    last.then_inc(sem("g_oT_ps"), 1)

                def gdn_act(act, h):
                    def W(name):
                        act.wait_ge(sem(name), h + 1)

                    def L(name, n, per_head):
                        act.wait_ge(sem(name), per_head * h + n)
                    yield 2
                    for a in range(3):
                        yield 2 + a
                        L("g_raw_ps", a + 1, 3)
                        nc.scalar.activation(ext[:, a, :, 3:], cvb[a][:, 0:TOK].rearrange("p (s q) -> p s q", q=NQ),
                                             ACT.Copy).then_inc(sem("g_ext"), 1)
                        nc.scalar.activation(cv[:, a, :], cvb[a][:, 0:TOK], ACT.Copy,
                                             scale=cw[:, bass.ds((TAP - 1) * 24 + a * 8 + h, 1)])\
                            .then_inc(sem("g_tap"), 1)
                    for a in range(3):
                        yield 5 + 3 * a
                        L("g_sum", a + 1, 3)
                        nc.scalar.activation(cvb[a][:, 0:TOK], cv[:, a, :], ACT.Tanh, scale=0.5)\
                            .then_inc(sem("g_th"), 1)
                    for a, bk in enumerate((b6, b7)):
                        yield 12 + 2 * a
                        L("g_tok_ps", a + 1, 3)
                        for t in range(TT):
                            last = nc.scalar.activation((qkd, qkdT)[a][:, t, :], tl(bk, t), ACT.Square, accum_out=nss[:, a, t:t + 1])
                        last.then_inc(sem("g_ss"), 1)
                    W("g_pol")
                    for t in range(TT):
                        last = nc.scalar.activation(nq[:, 0, t, :], tl(b6, t), ACT.Copy, scale=nrs[:, 0, t:t + 1])
                    last.then_inc(sem("g_nq"), 1)
                    yield 19
                    W("g_qT_ps")
                    nc.scalar.activation(qTn, b4[:, 0:TOK], ACT.Copy).then_inc(sem("g_qT"), 1)
                    yield 21
                    W("g_decin")
                    nc.scalar.activation(dec[:], dec[:], ACT.Exp).then_inc(sem("g_dec"), 1)
                    yield 22
                    W("g_ksT_ps")
                    nc.scalar.activation(ksT, b4[:, 0:2 * P].rearrange("p (a c) -> p a c", a=2), ACT.Copy)\
                        .then_inc(sem("g_ksT"), 1)
                    yield 24
                    W("g_U1_ps")
                    nc.scalar.activation(U[:], tiles(b5[:, 0:TOK]), ACT.Copy).then_inc(sem("g_U"), 1)
                    W("g_qkdT_ps")
                    nc.scalar.activation(qkdT[:], tiles(b3[:, 0:TOK]), ACT.Copy).then_inc(sem("g_qkdT"), 1)
                    for n in range(2, LEVELS):
                        yield GDN_LEVEL + 2 * n
                        m = n_tiles(n)
                        L("g_T_ps", n - 1, LEVELS - 2)
                        nc.scalar.activation(T[:, 0:m, :], tiles(b4[:, 0:m * P], m), ACT.Copy)\
                            .then_inc(sem("g_Tl"), 1)
                    act.wait_ge(sem("g_rows_out"), 16 * (NB + 1) * (h + 1))
                    nc.scalar.activation(zg, gbuf[:, :, 3 * HD:], ACT.Tanh, scale=0.5).then_inc(sem("g_thz"), 1)
                    yield 39
                    W("g_S1_ps")
                    nc.scalar.activation(S1[:], b4[:, 0:P], ACT.Copy).then_inc(sem("g_S1"), 1)
                    yield 48
                    W("g_oT_ps")
                    nc.scalar.activation(mixT_hi[:, bass.ds(h + HEADS, 1), :], b6[:, 0:TOK].unsqueeze(1), ACT.Copy,
                                         scale=nwg2[:]).then_inc(sem("g_mix_hi"), 1)

                def gdn_dve(dve, h):
                    V = nc.vector

                    def W(name):
                        dve.wait_ge(sem(name), h + 1)

                    def L(name, n, per_head):
                        dve.wait_ge(sem(name), per_head * h + n)

                    own = [0]

                    def after(ins):
                        own[0] += 1
                        ins.then_inc(sem("g_own"), 1)
                        L("g_own", own[0], G_OWN)

                    def col(x, t):
                        return x[:, t, bass.ds(h, 1)]
                    yield 0
                    V.tensor_scalar(ngh, nGT[:], cn[0:HEADS, bass.ds(C_ID + h, 1)], None, ALU.mult)\
                        .then_inc(sem("g_ngh"), 1)
                    for a in range(3):
                        yield 2 + 3 * a
                        L("g_ext", a + 1, 3), L("g_pre", a + 1, 3), L("g_tap", a + 1, 3)
                        out = cv[:, a, :].rearrange("p (s q) -> p s q", q=NQ)
                        for r in range(TAP - 1):
                            w = cw[:, bass.ds(r * 24 + a * 8 + h, 1)]
                            ins = V.scalar_tensor_tensor(out=out, in0=ext[:, a, :, r:r + NQ], scalar=w, in1=out,
                                                         op0=ALU.mult, op1=ALU.add)
                            if r < TAP - 2:
                                after(ins)
                            else:
                                ins.then_inc(sem("g_sum"), 1)
                        if a > 0:
                            silu(dve, h, a - 1)
                    yield 11
                    silu(dve, h, 2)
                    yield 14
                    L("g_ss", 2, 2)
                    for a, f in ((0, 1.0 * HD), (1, 1.0)):
                        ins = V.tensor_scalar(nss[:, a, :], nss[:, a, :], f, 4e-6 * f, ALU.mult, ALU.add)
                    after(ins)
                    rsqrt(nrs[:], nss[:], npol[:], after)
                    dve.sem_inc(sem("g_pol"), 1)
                    for t in range(TT):
                        ins = V.tensor_scalar(nq[:, 1, t, :], tl(b7, t), nrs[:, 1, t:t + 1], None, ALU.mult)
                    ins.then_inc(sem("g_nk"), 1)
                    yield 17
                    L("g_tok_ps", 3, 3)
                    for t in range(TT):
                        ins = V.tensor_scalar(nq[:, 2, t, :], tl(b3, t), col(bhalf, t), None, ALU.mult)
                    ins.then_inc(sem("g_nv"), 1)
                    yield 19
                    W("g_kT_ps")
                    V.tensor_copy(kTn, b5[:, 0:TOK]).then_inc(sem("g_kT"), 1)
                    yield 21
                    W("g_dec_ps")
                    for t in range(TT):
                        m = C_MP if t < 2 else C_MS
                        ins = V.scalar_tensor_tensor(out=dec[:, t, :], in0=tl(b3, t), scalar=col(Gc, t),
                                                     in1=cn[:, m + P:m + 2 * P], op0=ALU.add, op1=ALU.add)
                    ins.then_inc(sem("g_decin"), 1)
                    W("g_dec"), W("g_kk_ps")
                    for t in range(TT):
                        ins = V.scalar_tensor_tensor(out=A[:, t, :], in0=tl(b6, t), scalar=col(beta, t),
                                                     in1=dec[:, t, :], op0=ALU.mult, op1=ALU.mult)
                    after(ins)
                    after(V.tensor_tensor(B, A, lv[0].unsqueeze(1).broadcast_to([P, TT, P]), ALU.mult))
                    V.tensor_tensor(T, ident.unsqueeze(1).broadcast_to([P, TT, P]), B, ALU.subtract)\
                        .then_inc(sem("g_T1"), 1)
                    W("g_qk_ps")
                    V.tensor_tensor(qkd[:], tiles(b7[:, 0:TOK]), dec[:], ALU.mult).then_inc(sem("g_qkd"), 1)
                    W("g_T1")
                    V.tensor_tensor(B, A, lv[1].unsqueeze(1).broadcast_to([P, TT, P]), ALU.mult)\
                        .then_inc(sem("g_B"), 1)
                    yield 24
                    W("g_ks_ps")
                    V.scalar_tensor_tensor(out=R[:, 2, :], in0=b7[:, 0:P], scalar=col(nbe, 2), in1=nq[:, 2, 2, :],
                                           op0=ALU.mult, op1=ALU.add).then_inc(sem("g_R2"), 1)
                    V.tensor_scalar(oq[:, 2, :], b7[:, P:2 * P], col(eG, 2), None, ALU.mult).then_inc(sem("g_oq2"), 1)
                    for n in range(1, LEVELS):
                        yield GDN_LEVEL + 2 * n
                        m = n_tiles(n)
                        L("g_Z_ps", n, LEVELS - 1)
                        V.tensor_copy(Z[:, 0:m, :], tiles(b6[:, 0:m * P], m)).then_inc(sem("g_Z"), 1)
                        if n + 1 < LEVELS:
                            V.tensor_tensor(B, A, lv[n + 1].unsqueeze(1).broadcast_to([P, TT, P]), ALU.mult)\
                                .then_inc(sem("g_B"), 1)
                        yield GDN_LEVEL + 2 * n + 1
                        L("g_UZ_ps", n, LEVELS - 1), L("g_U", n, LEVELS)
                        V.tensor_tensor(U[:, 0:m, :], U[:, 0:m, :], tiles(b5[:, 0:m * P], m), ALU.subtract)\
                            .then_inc(sem("g_U"), 1)
                    yield 38
                    W("g_v02_ps")
                    V.tensor_copy(vn[:, 0, :], tl(b6, 0))
                    V.tensor_copy(vn[:, 2, :], tl(b6, 2)).then_inc(sem("g_v02"), 1)
                    yield 40
                    W("g_ks1_ps")
                    V.scalar_tensor_tensor(out=R[:, 1, :], in0=b5[:, 0:P], scalar=col(nbe, 1), in1=nq[:, 2, 1, :],
                                           op0=ALU.mult, op1=ALU.add)
                    V.tensor_scalar(oq[:, 1, :], b5[:, P:2 * P], col(eG, 1), None, ALU.mult).then_inc(sem("g_R1"), 1)
                    yield 41
                    W("g_v1_ps")
                    V.tensor_copy(vn[:, 1, :], tl(b6, 0)).then_inc(sem("g_v1"), 1)
                    yield 42
                    W("g_o_ps"), W("g_oq2")
                    V.tensor_copy(go[:, 0, :], tl(b7, 0))
                    after(V.tensor_tensor(go[:, 1:3, :], oq[:, 1:3, :], tiles(b7[:, P:3 * P], 2), ALU.add))
                    for t in range(TT):
                        ins = V.scalar_tensor_tensor(out=R[:, t, :], in0=go[:, t, :], scalar=1.0, in1=go[:, t, :],
                                                     op0=ALU.mult, op1=ALU.mult, accum_out=gss[:, t:t + 1])
                    after(ins)
                    after(V.tensor_scalar(gss[:], gss[:], 1.0 / HD, 1e-6, ALU.mult, ALU.add))
                    rsqrt(grs[:], gss[:], pol[:], after)
                    W("g_zg")
                    for t in range(TT):
                        ins = V.scalar_tensor_tensor(out=go[:, t, :], in0=go[:, t, :], scalar=grs[:, t:t + 1],
                                                     in1=zg[:, t, :], op0=ALU.mult, op1=ALU.mult)
                    ins.then_inc(sem("g_o"), 1)
                    W("g_S2_ps"), W("g_S1")
                    V.scalar_tensor_tensor(out=S1[:], in0=S1[:], scalar=eL[:, 1, bass.ds(h, 1)], in1=b4[:, 0:P],
                                           op0=ALU.mult, op1=ALU.add)
                    W("g_Ss_ps"), W("g_Sdec")
                    V.tensor_tensor(S[:, 0:4, :], S[:, 0:4, :], tiles(b3[:, :], 4), ALU.add)
                    V.tensor_tensor(S[:, 4:8, :], S[:, 4:8, :], tiles(b5[:, :], 4), ALU.add)\
                        .then_inc(sem("g_state"), 1)
                    yield 48
                    W("g_mix_hi")
                    V.scalar_tensor_tensor(out=mixT_lo[:, bass.ds(h + HEADS, 1), :], in0=b6[:, 0:TOK].unsqueeze(1),
                                           scalar=nwg2[:], in1=mixT_hi[:, bass.ds(h + HEADS, 1), :], op0=ALU.mult,
                                           op1=ALU.subtract).then_inc(sem("g_mix"), 1)
                    assert own[0] == G_OWN

                def silu(dve, h, a):
                    dve.wait_ge(sem("g_th"), 3 * h + a + 1)
                    nc.vector.scalar_tensor_tensor(out=cv[:, a, :], in0=cvb[a][:, 0:TOK], scalar=1.0,
                                                   in1=cv[:, a, :], op0=ALU.add, op1=ALU.mult)\
                        .then_inc(sem("g_cv"), 1)

                def gdn_pool(pool, h):
                    G = nc.gpsimd

                    def W(name):
                        pool_wait(pool, sem(name), h + 1)
                    for a in range(3):
                        pool_wait(pool, sem("g_ext"), 3 * h + a + 1)
                        if a == 0:
                            G.memset(ext[:, :, 0, 0:3], 0.0)
                        G.tensor_copy(ext[:, a, 1:2 * P // NQ, 0:3], ext[:, a, 0:2 * P // NQ - 1, NQ:NQ + 3])
                        G.tensor_copy(ext[:, a, 2 * P // NQ:, 0:3],
                                      cprev[:, bass.ds(a * 8 + h, 1), :].rearrange("p o (b r) -> p (o b) r", r=3))\
                            .then_inc(sem("g_pre"), 1)
                    pool_wait(pool, sem("g_buf"), TT * (h + 1))
                    pool.dma_start(o_cp[0, 0].rearrange("r (a g c) -> r a g c", a=3, c=HD)[:, :, bass.ds(h, 1), :]
                                   .rearrange("r a o c -> r a (o c)"),
                                   gbuf[P - 3:P, 1, 0:3 * HD].rearrange("p (a c) -> p a c", a=3))\
                        .then_inc(sem("g_rows_out"), 16)
                    for b in range(NB):
                        pool.dma_start(
                            o_cs[0, b].rearrange("r (a g c) -> r a g c", a=3, c=HD)[:, :, bass.ds(h, 1), :]
                            .rearrange("r a o c -> r a (o c)"),
                            gbuf[(b + 1) * NQ - 3:(b + 1) * NQ, 2, 0:3 * HD].rearrange("p (a c) -> p a c", a=3))\
                            .then_inc(sem("g_rows_out"), 16)
                    W("g_nk")
                    G.tensor_tensor(ke[:], nq[:, 1], per_token(eR, h), ALU.mult).then_inc(sem("g_ke"), 1)
                    W("g_ksT_ps")
                    G.tensor_tensor(S[:], S[:], per_token(eL[:, 2:, :], h, NB), ALU.mult).then_inc(sem("g_Sdec"), 1)
                    W("g_thz")
                    G.tensor_scalar(zg, zg, 1.0, None, ALU.add).then_inc(sem("g_zg1"), 1)
                    W("g_zg1")
                    G.tensor_tensor(zg, zg, gbuf[:, :, 3 * HD:], ALU.mult).then_inc(sem("g_zg"), 1)
                    W("g_v02")
                    G.tensor_tensor(vm[:], vn[:, 2, :].unsqueeze(1).broadcast_to([P, NB, HD]),
                                    cn[:, C_BM:C_BM + NB].unsqueeze(2).broadcast_to([P, NB, HD]), ALU.mult)\
                        .then_inc(sem("g_vm"), 1)

                def load_state(eng, h):
                    eng.dma_start(S[:], state_gdn[0, :, bass.ds(h, 1)].rearrange("b o k v -> k b (o v)"))\
                        .then_inc(sem("g_S_in"), 16)

                def store_state(eng, h):
                    eng.wait_ge(sem("g_state"), h + 2)
                    eng.dma_start(o_sp[0, 0, bass.ds(h, 1)].rearrange("o k v -> (o k) v"), S1[:])\
                        .then_inc(sem("g_S_out"), 16)
                    eng.dma_start(o_ss[0, :, bass.ds(h, 1)].rearrange("b o k v -> k b (o v)"), S[:])\
                        .then_inc(sem("g_S_out"), 16)

                def next_state(eng, n, h):
                    if n == STORE_AT:
                        store_state(eng, h)
                    if n == STORE_AT + 2:
                        eng.wait_ge(sem("g_S_out"), 32 * (h + 1))
                        load_state(eng, h + 1)

                @block.sync
                def _(sp):
                    load_state(sp, 0)
                    for n in range(RAW + A_DVE, NP_IN):
                        loads(sp, G_GDN + NP_IN + n, n % RAW, gdn_parts(1, n, n % RAW))
                    with sp.Fori(0, HEADS - 2) as i:
                        for n in range(NP_IN):
                            next_state(sp, n, i)
                            loads(sp, G_GDN + 2 * NP_IN + n + NP_IN * i, n % RAW, gdn_parts(i + 2, n, n % RAW))
                    for n in range(NCB * NP_HALF):
                        c, m = divmod(n, NP_HALF)
                        next_state(sp, n, HEADS - 2)
                        loads(sp, G_OUT_FOX + n, n % RAW, plain_parts(w_out, m * P, c * CW, n % RAW,
                                                                      dmas_of(G_OUT_FOX + n)))
                    with sp.Fori(0, NCB) as c:
                        for n in range(NP_HALF):
                            loads(sp, G_OUT_GDN + n + NP_HALF * c, n % RAW,
                                  plain_parts(w_out, (NP_HALF + n) * P, c * CW, n % RAW))
                    for n in range(RAW + A_DVE):
                        loads(sp, G_UP0 + n, n % RAW, plain_parts(w_gate, n * P, 0, n % RAW))
                    store_state(sp, HEADS - 1)
                    sp.wait_ge(sem("g_S_out"), 32 * HEADS)
                    sp.wait_ge(sem("g_mix"), HEADS + 1)
                    load_gb(sp, gb, ln_mix_g[0], ln_mix_b[0])
                    sp.wait_ge(sem("g_rows_out"), 16 * (NB + 1) * HEADS)

                @block.gpsimd
                def _(pool):
                    with pool.Fori(0, HEADS) as i:
                        gdn_pool(pool, i)

                @block.scalar
                def _(act):
                    with act.Fori(0, HEADS - 1) as i:
                        act_block(act, G_GDN + NP_IN, i, NP_IN, Course(gdn_act(act, i)), lambda t: (
                            act.wait_ge(sem("g_o"), i + 1), gdn_evac(act, i + 1, t)))
                    mixer = Course(gdn_act(act, HEADS - 1))
                    for n in range(NCB * NP_HALF):
                        mixer.upto(SLOTS * n + SLOTS - 1)
                        split_act(act, G_OUT_FOX + A_ACT, n)
                    with act.Fori(0, NCB) as c:
                        for n in range(NP_HALF):
                            split_act(act, G_OUT_GDN + A_ACT, n, c, NP_HALF)

                def stats_of_block(dve, c, acc_free):
                    dve.wait_ge(sem("acc_free"), acc_free)
                    for t in range(TT):
                        last = row_stats(t, c)
                    return last

                def out_evac(dve, blk, c, t, scale):
                    wait_acc(dve, "acc", blk, t, G_OUT_FOX + NP_HALF * (blk - 2 * HEADS + 1))
                    xs = x_res[:, t, bass.ds(c * CW, CW)]
                    nc.vector.scalar_tensor_tensor(out=xs, in0=xs, scalar=scale, in1=bank[t][:, :], op0=ALU.mult,
                                                   op1=ALU.add).then_inc(sem("acc_free"), 1)

                @block.vector
                def _(dve):
                    dve.sem_inc(sem("g_state"), 1)
                    dve.sem_inc(sem("g_mix"), 1)
                    with dve.Fori(0, HEADS - 1) as i:
                        dve_block(dve, G_GDN + NP_IN, i, NP_IN, Course(gdn_dve(dve, i)))
                    mixer = Course(gdn_dve(dve, HEADS - 1))
                    for n in range(NCB * NP_HALF):
                        c, m = divmod(n, NP_HALF)
                        mixer.upto(SLOTS * n + SLOTS - 1)
                        split_dve(dve, G_OUT_FOX + A_DVE, n)
                        if m == NP_HALF - 1:
                            for t in range(TT):
                                out_evac(dve, 2 * HEADS + c, c, t, ALPHA)
                    with dve.Fori(0, NCB) as c:
                        for n in range(NP_HALF):
                            split_dve(dve, G_OUT_GDN + A_DVE, n, c, NP_HALF)
                        for t in range(TT):
                            out_evac(dve, 2 * HEADS + NCB + c, c, t, 1.0)
                        stats_of_block(dve, c, TT * (2 * HEADS + NCB + 1 + c)).then_inc(sem("x_stats"), 1)
                    dve.wait_ge(sem("x_stats"), NCB)

                @block.tensor
                def _(pe):
                    with pe.Fori(0, HEADS - 1) as i:
                        gemm(pe, G_GDN + NP_IN, NP_IN, aT_hi, aT_lo, 0, CW, ACC, "acc", HEADS + 1, i, NP_IN, 1,
                             Course(gdn_pe(pe, i)))
                    mixer = Course(gdn_pe(pe, HEADS - 1))
                    for c in range(NCB):
                        gemm(pe, G_OUT_FOX + NP_HALF * c, NP_HALF, mixT_hi, mixT_lo, 0, CW, ACC, "acc",
                             2 * HEADS + c, between=mixer, ends=c == NCB - 1, slot0=SLOTS * NP_HALF * c)
                    pe.wait_ge(sem("g_mix"), HEADS + 1)
                    with pe.Fori(0, NCB) as c:
                        gemm(pe, G_OUT_GDN, NP_HALF, mixT_hi, mixT_lo, HEADS, CW, ACC, "acc", 2 * HEADS + NCB, c,
                             NP_HALF, 1)

            with ExitStack() as ctx:
                block = ctx.enter_context(nc.Block())

                @block.gpsimd
                def _(pool):
                    for r in range(ROUNDS):
                        shift_pool(pool, r, gb, 1)

                @block.scalar
                def _(act):
                    for r in range(ROUNDS + LAG):
                        if r < ROUNDS:
                            normalise_act(act, r, 1, TT + 1 if r == 0 else None)
                        if r >= LAG:
                            x_evac_act(act, r - LAG, 1)

                @block.vector
                def _(dve):
                    moments_dve(dve, range(TT))
                    for r in range(ROUNDS + LAG):
                        if r < ROUNDS:
                            scale_dve(dve, r, gb, 1)
                        if r >= LAG:
                            x_evac_dve(dve, r - LAG, 1)

                @block.tensor
                def _(pe):
                    for r in range(ROUNDS):
                        x_transpose_pe(pe, r, 1)
        BLK_MIX = 2 * HEADS + 2 * NCB

        with ExitStack() as ctx:
            hT_hi = sb(ctx, "hT_hi", [P, KH, TOK], F32R)
            hT_lo = sb(ctx, "hT_lo", [P, KH, TOK], F32R)
            sg = sb(ctx, "sg", [P, TT, CW])
            hb = sb(ctx, "hb", [P, TT, CW])
            block = ctx.enter_context(nc.Block())

            def stream(g0, i):
                return (g0 + 2 * NP_IN * i, 0, 0) if isinstance(i, int) else (g0, i, 2 * NP_IN)

            def gate_block(j0):
                return BLK_MIX + j0 + (NCB if j0 else 0)

            def four(b):
                return b[:, :].rearrange("p (k c) -> p k c", k=4)

            def gate_pe(pe, g0, j0, i, between=None, ahead=0):
                g, ii, per = stream(g0, i)
                blk = gate_block(j0) + ahead + (i if per == 0 else 0)
                gemm(pe, g + 2 * NP_IN * ahead, NP_IN, aT_hi, aT_lo, 0, CW, ACC, "acc", blk, ii, per, 1, between)

            def up_pe(pe, g0, j0, i):
                g, ii, per = stream(g0, i)
                gemm(pe, g + NP_IN, NP_IN, aT_hi, aT_lo, 0, CW, ACC2, "acc2", j0 + 1 + (i if per == 0 else 0), ii,
                     per, 1)

            def hidden_pe(pe, j, last=False):
                for t in range(TT):
                    yield HIDDEN_AT[t]
                    pe.wait_ge(sem("h_ready"), TT * j + t + 1)
                    pe.wait_ge(sem("h_bank"), TT * j + t + 1)
                    for k in range(4):
                        ins = nc.tensor.transpose(bank[6 + t % 2][:, k * P:(k + 1) * P],
                                                  hb[:, t, k * P:(k + 1) * P], ident)
                    ins.then_inc(sem("h_ps"), 1)
                if last:
                    yield 40
                    pe.wait_ge(sem("h_bank"), 2 + TT * (j + 1))

            def hidden_act(act, i, j):
                for t in range(TT):
                    yield HIDDEN_AT[t]
                    act.wait_ge(sem("h_ps"), TT * j + t + 1)
                    nc.scalar.activation(hT_hi[:, bass.ds(4 * i, 4), t * P:(t + 1) * P], four(bank[6 + t % 2]),
                                         ACT.Copy).then_inc(sem("h_hi"), 1)

            def hidden_dve(dve, i, j):
                for t in range(TT):
                    yield HIDDEN_AT[t]
                    dve.wait_ge(sem("h_hi"), TT * j + t + 1)
                    ks, cs = bass.ds(4 * i, 4), slice(t * P, (t + 1) * P)
                    nc.vector.tensor_tensor(hT_lo[:, ks, cs], four(bank[6 + t % 2]), hT_hi[:, ks, cs],
                                            ALU.subtract).then_inc(sem("h_bank"), 1)

            def up_act(act, g0, j0, i):
                for t in range(TT):
                    wait_acc(act, "acc", gate_block(j0) + i, t, g0 + NP_IN + 2 * NP_IN * i)
                    nc.scalar.activation(sg[:, t, :], bank[t][:, :], ACT.Tanh, scale=0.5)\
                        .then_inc(sem("sg_tanh"), 1)
                g, ii, per = stream(g0, i)
                for n in range(NP_IN):
                    split_act(act, g + NP_IN + A_ACT, n, ii, per)

            def up_dve(dve, g0, j0, i):
                j = j0 + i
                for t in range(TT):
                    dve.wait_ge(sem("sg_tanh"), TT * j + t + 1)
                    nc.vector.scalar_tensor_tensor(out=sg[:, t, :], in0=sg[:, t, :], scalar=1.0,
                                                   in1=bank[t][:, :], op0=ALU.add, op1=ALU.mult)\
                        .then_inc(sem("acc_free"), 1)
                g, ii, per = stream(g0, i)
                for n in range(NP_IN):
                    split_dve(dve, g + NP_IN + A_DVE, n, ii, per)
                dve.wait_ge(sem("acc_free"), TT * (gate_block(j0) + i) + TT)
                for t in range(TT):
                    wait_acc(dve, "acc2", j, t, g0 + 2 * NP_IN + 2 * NP_IN * i)
                    nc.vector.scalar_tensor_tensor(out=hb[:, t, :], in0=bank[3 + t][:, :], scalar=0.5,
                                                   in1=sg[:, t, :], op0=ALU.mult, op1=ALU.mult)\
                        .then_inc(sem("h_ready"), 1)
                dve.wait_ge(sem("h_ready"), TT * j + TT)
                dve.sem_inc(sem("acc2_free"), TT)

            def splits_beside(split, eng, ahead, g, pieces, i=0, per=0, course=None, end=None):
                for n in range(pieces):
                    if course is not None:
                        course.upto(SLOTS * n + SLOTS - 1)
                    if end is None or g + ahead + n < end:
                        split(eng, g + ahead, n, i, per)
                if course is not None:
                    course.upto(None)

            def down_evac(dve, half, c, t, blk):
                wait_acc(dve, "acc", blk, t, (G_DN0, G_DN1)[half] + NP_DN[half] * (c + 1))
                xs = x_res[:, t, bass.ds(c * CW, CW)]
                nc.vector.scalar_tensor_tensor(out=xs, in0=xs, scalar=(ALPHA if half == 0 else 1.0),
                                               in1=bank[t][:, :], op0=ALU.mult, op1=ALU.add)\
                    .then_inc(sem("acc_free"), 1)
            BLK_DN = (BLK_MIX + FB[0], BLK_MIX + FB[0] + NCB + FB[1])

            @block.sync
            def _(sp):
                def up_loads(g0, j0, i, skip):
                    for n in range(skip, 2 * NP_IN):
                        w, m = (w_gate, n) if n < NP_IN else (w_up, n - NP_IN)
                        per = 0 if isinstance(i, int) else 2 * NP_IN
                        loads(sp, g0 + n + per * (i if per else 0), n % RAW,
                              plain_parts(w, m * P, (j0 + i) * CW, n % RAW))

                def down_loads(g0, half, c, per):
                    for n in range(NP_DN[half]):
                        slot = (g0 + n) % RAW
                        loads(sp, g0 + n + per * (c if per else 0), slot,
                              plain_parts(w_down, (half * NP_DN[0] + n) * P, c * CW, slot))
                up_loads(G_UP0, 0, 0, RAW + A_DVE)
                with sp.Fori(0, FB[0] - 1) as i:
                    up_loads(G_UP0 + 2 * NP_IN, 1, i, 0)
                with sp.Fori(0, NCB) as c:
                    down_loads(G_DN0, 0, c, NP_DN[0])
                with sp.Fori(0, FB[1]) as i:
                    up_loads(G_UP1, FB[0], i, 0)
                for c in range(NCB):
                    down_loads(G_DN1 + NP_DN[1] * c, 1, c, 0)
                sp.wait_ge(sem("w_split"), G_END)
                load_gb(sp, gb_last, ln_ffn_g[0], ln_ffn_b[0])

            @block.scalar
            def _(act):
                def half(n, g0, j0):
                    splits_beside(split_act, act, A_ACT, g0, NP_IN)
                    with act.Fori(0, FB[n] - 1) as i:
                        up_act(act, g0, j0, i)
                        splits_beside(split_act, act, A_ACT, g0 + 2 * NP_IN, NP_IN, i, 2 * NP_IN,
                                      Course(hidden_act(act, i, j0 + i)))
                    up_act(act, g0, j0, FB[n] - 1)
                half(0, G_UP0, 0)
                splits_beside(split_act, act, A_ACT, G_DN0, NP_DN[0], course=Course(hidden_act(act, FB[0] - 1, FB[0] - 1)))
                with act.Fori(1, NCB) as c:
                    splits_beside(split_act, act, A_ACT, G_DN0, NP_DN[0], c, NP_DN[0])
                half(1, G_UP1, FB[0])
                splits_beside(split_act, act, A_ACT, G_DN1, NP_DN[1] * NCB,
                              course=Course(hidden_act(act, FB[1] - 1, FB[0] + FB[1] - 1)), end=G_END)

            @block.vector
            def _(dve):
                dve.sem_inc(sem("h_bank"), 2)
                dve.sem_inc(sem("acc2_free"), TT)

                def half(n, g0, j0):
                    splits_beside(split_dve, dve, A_DVE, g0, NP_IN)
                    with dve.Fori(0, FB[n] - 1) as i:
                        up_dve(dve, g0, j0, i)
                        splits_beside(split_dve, dve, A_DVE, g0 + 2 * NP_IN, NP_IN, i, 2 * NP_IN,
                                      Course(hidden_dve(dve, i, j0 + i)))
                    up_dve(dve, g0, j0, FB[n] - 1)

                def down_block(n, g, c, i=0, per=0, course=None, end=None):
                    splits_beside(split_dve, dve, A_DVE, g, NP_DN[n], i, per, course, end)
                    for t in range(TT):
                        down_evac(dve, n, c, t, BLK_DN[n] + c)
                half(0, G_UP0, 0)
                down_block(0, G_DN0, 0, course=Course(hidden_dve(dve, FB[0] - 1, FB[0] - 1)))
                with dve.Fori(1, NCB) as c:
                    down_block(0, G_DN0, c, c, NP_DN[0])
                half(1, G_UP1, FB[0])
                for c in range(NCB):
                    down_block(1, G_DN1 + c * NP_DN[1], c, end=G_END, course=(
                        Course(hidden_dve(dve, FB[1] - 1, FB[0] + FB[1] - 1)) if c == 0 else None))
                    dve.wait_ge(sem("acc_free"), TT * (BLK_DN[1] + c + 1))
                    for t in range(TT):
                        last = row_stats(t, c)
                link(dve, last)

            @block.tensor
            def _(pe):
                def half(n, g0, j0):
                    gate_pe(pe, g0, j0, 0)
                    with pe.Fori(0, FB[n] - 1) as i:
                        up_pe(pe, g0, j0, i)
                        gate_pe(pe, g0, j0, i, Course(hidden_pe(pe, j0 + i)), ahead=1)
                    up_pe(pe, g0, j0, FB[n] - 1)
                half(0, G_UP0, 0)
                gemm(pe, G_DN0, NP_DN[0], hT_hi, hT_lo, 0, CW, ACC, "acc", BLK_DN[0],
                     between=Course(hidden_pe(pe, FB[0] - 1, True)))
                with pe.Fori(1, NCB) as c:
                    gemm(pe, G_DN0, NP_DN[0], hT_hi, hT_lo, 0, CW, ACC, "acc", BLK_DN[0], c, NP_DN[0], 1)
                half(1, G_UP1, FB[0])
                for c in range(NCB):
                    gemm(pe, G_DN1 + NP_DN[1] * c, NP_DN[1], hT_hi, hT_lo, 0, CW, ACC, "acc", BLK_DN[1] + c,
                         between=Course(hidden_pe(pe, FB[0] + FB[1] - 1, True)) if c == 0 else None)

        with ExitStack() as ctx:
            block = ctx.enter_context(nc.Block())

            @block.sync
            def _(sp):
                for r in range(ROUNDS):
                    sp.wait_ge(sem("ln_done"), ROUNDS * 2 + r + 1)
                    t, x, c = quarter(r)
                    dst = y_prompt[0, t * P:(t + 1) * P, :] if t < 2 else y_sample.rearrange("b s d -> (b s) d")
                    sp.dma_start(dst[:, c], x).then_inc(sem("y_stored"), 16)
                sp.wait_ge(sem("y_stored"), 16 * ROUNDS)

            @block.scalar
            def _(act):
                for r in range(ROUNDS):
                    normalise_act(act, r, 2, TT + 2 if r == 0 else None)

            @block.vector
            def _(dve):
                moments_dve(dve, range(TT))
                for r in range(ROUNDS):
                    scale_dve(dve, r, gb_last, 2)

            @block.gpsimd
            def _(pool):
                for r in range(ROUNDS):
                    shift_pool(pool, r, gb_last, 2)


_INS = ["x_prompt", "x_sample", "cache_fox_k", "cache_fox_v", "cache_fox_logf", "state_gdn", "state_gdn_conv",
        "ln_in_g", "ln_in_b", "w_in", "fox_f_bias", "fox_norm_w", "gdn_conv_w", "gdn_a_log", "gdn_dt_bias",
        "gdn_norm_w", "w_out", "ln_mix_g", "ln_mix_b", "ffn_w_gate", "ffn_w_up", "ffn_w_down", "ln_ffn_g",
        "ln_ffn_b"]
_OUTS = [(1, 256, D), (NB, NQ, D),
         (1, 1, 256, HEADS, HD), (1, 1, 256, HEADS, HD), (1, 1, 256, HEADS), (1, 1, HEADS, HD, HD), (1, 1, 3, 3072),
         (1, NB, NQ, HEADS, HD), (1, NB, NQ, HEADS, HD), (1, NB, NQ, HEADS), (1, NB, HEADS, HD, HD),
         (1, NB, 3, 3072)]


def kernel(**inputs):
    import concourse.bacc as _bacc
    from concourse.bass_utils import run_bass_kernel_spmd as _run

    nc = _bacc.Bacc("TRN2", target_bir_lowering=False, num_devices=1)
    arrays, args = {}, []
    for name in _INS + ["constants"]:
        a = constants() if name == "constants" else np.ascontiguousarray(inputs[name])
        arrays[f"in_{name}"] = a
        args.append(nc.dram_tensor(f"in_{name}", a.shape, mybir.dt.from_np(a.dtype), kind="ExternalInput").ap())
    for i, shape in enumerate(_OUTS):
        args.append(nc.dram_tensor(f"out_{i}", shape, F32, kind="ExternalOutput").ap())
    encoder_layer(nc, *args)
    r = _run(nc, [arrays], core_ids=[0])
    return tuple(r.results[0][f"out_{i}"] for i in range(len(_OUTS)))
```
